# Optimizing a Trainium2 kernel written in Bass

```python
import jax, jax.numpy as jnp
from jax import lax
import numpy as np

D_MODEL = 1024
BATCH = 1
SEQ = 1024
DEPTH = 2
DEC_BATCH = 1
DEC_SEQ = 32
PAST_LEN = 256

CHUNK = 64
A_CHUNK = 128
D_A = D_MODEL // 2
A_HEADS = 4
A_HEAD_DIM = D_A // A_HEADS
D_B = D_MODEL // 2
B_HEADS = 8
B_HEAD_DIM = D_B // B_HEADS
B_CONV = 4
LRU_C = 8.0
D_C = D_MODEL
C_CONV = 3
D_FF = 4 * D_MODEL
N_EVEN = (DEPTH + 1) // 2
N_ODD = DEPTH // 2
D_IN_EVEN = 2 * D_A + 2 * D_B
EPS = 1e-6

kernel_name = "hybrid_gmlp_rglru_shortconv_stream_step"

def rmsnorm(x, g):
    xf = x.astype(jnp.float32)
    y = xf * lax.rsqrt(jnp.mean(xf * xf, axis=-1, keepdims=True) + EPS)
    return (y * g.astype(jnp.float32)).astype(x.dtype)

def causal_dwconv(x, buf, w):
    width = w.shape[0]
    T = x.shape[1]
    xf = jnp.concatenate([buf.astype(x.dtype), x], axis=1)
    y = w[0] * xf[:, 0:T]
    for k in range(1, width):
        y = y + w[k] * xf[:, k:k + T]
    return y, xf[:, -(width - 1):]

def spatial_gating(u, v, w_s, b_s):
    bsz, T, _ = v.shape
    L = min(T, A_CHUNK)
    n = T // L
    pos = jnp.arange(L)
    mask = (pos[None, :] // CHUNK) <= (pos[:, None] // CHUNK)
    w = jnp.where(mask[None], w_s[:, :L, :L], 0).astype(v.dtype)
    vc = v.reshape(bsz, n, L, A_HEADS, A_HEAD_DIM)
    s = jnp.einsum('hij,bnjhc->bnihc', w, vc) + b_s[:, :L].T[None, None, :, :, None].astype(v.dtype)
    return u * s.reshape(bsz, T, D_A)

def rg_lru(x, h0, wa, ba, wx, bx, lam):
    bsz, T, _ = x.shape
    xh = x.reshape(bsz, T, B_HEADS, B_HEAD_DIM)
    r = jax.nn.sigmoid((jnp.einsum('bthi,hij->bthj', xh, wa).reshape(bsz, T, D_B) + ba).astype(jnp.float32))
    ig = jax.nn.sigmoid((jnp.einsum('bthi,hij->bthj', xh, wx).reshape(bsz, T, D_B) + bx).astype(jnp.float32))
    log_a = -LRU_C * r * jax.nn.softplus(-lam.astype(jnp.float32))
    a = jnp.exp(log_a)
    bterm = jnp.sqrt(-jnp.expm1(2.0 * log_a)) * ig * x.astype(jnp.float32)

    def combine(p, q):
        a1, b1 = p
        a2, b2 = q
        return a1 * a2, a2 * b1 + b2

    a_cum, b_cum = lax.associative_scan(combine, (a, bterm), axis=1)
    h = b_cum + a_cum * h0.astype(jnp.float32)[:, None]
    return h.astype(x.dtype), h[:, -1].astype(x.dtype)

def mixer_even(h, conv_buf, h0, w_in, v_gain, w_s, b_s, conv_w, conv_b, wa, ba, wx, bx, lam, w_out):
    z = h @ w_in
    u, v, xb, gb = jnp.split(z, [D_A, 2 * D_A, 2 * D_A + D_B], axis=-1)
    u = jax.nn.gelu(u)
    v = rmsnorm(jax.nn.gelu(v), v_gain)
    a_out = spatial_gating(u, v, w_s, b_s)
    xc, new_buf = causal_dwconv(xb, conv_buf, conv_w)
    hr, h_last = rg_lru(xc + conv_b, h0, wa, ba, wx, bx, lam)
    b_out = hr * jax.nn.gelu(gb)
    out = jnp.concatenate([a_out, b_out], axis=-1) @ w_out
    return out, v, new_buf, h_last

def mixer_odd(h, conv_buf, w_in, conv_w, w_out):
    bg, cg, xv = jnp.split(h @ w_in, 3, axis=-1)
    y, new_buf = causal_dwconv(cg * xv, conv_buf, conv_w)
    return (bg * y) @ w_out, new_buf

def trunk(x, b_conv, b_h, c_conv, p):
    v_rows, b_conv_new, b_h_new, c_conv_new = [], [], [], []
    for l in range(DEPTH):
        hn = rmsnorm(x, p['norm_mix_pre'][l])
        if l % 2 == 0:
            e = l // 2
            m, v, bc, bh = mixer_even(hn, b_conv[e], b_h[e], p['w_in_even'][e], p['a_v_gain'][e],
                                      p['a_w_s'][e], p['a_b_s'][e], p['b_conv_w'][e], p['b_conv_b'][e],
                                      p['b_wa'][e], p['b_ba'][e], p['b_wx'][e], p['b_bx'][e],
                                      p['b_lambda'][e], p['w_out_even'][e])
            v_rows.append(v)
            b_conv_new.append(bc)
            b_h_new.append(bh)
        else:
            o = l // 2
            m, cc = mixer_odd(hn, c_conv[o], p['c_w_in'][o], p['c_conv_w'][o], p['c_w_out'][o])
            c_conv_new.append(cc)
        x = x + rmsnorm(m, p['norm_mix_post'][l])
        hn = rmsnorm(x, p['norm_ffn_pre'][l])
        f = jnp.square(jax.nn.relu(hn @ p['mlp_up'][l])) @ p['mlp_down'][l]
        x = x + rmsnorm(f, p['norm_ffn_post'][l])
    return x, jnp.stack(v_rows), jnp.stack(b_conv_new), jnp.stack(b_h_new), jnp.stack(c_conv_new)

def setup_inputs(seed: int = 0) -> dict:
    key = jax.random.key(seed)
    ks = jax.random.split(key, 32)
    nrm = lambda k, shape, s: jax.random.normal(k, shape, jnp.float32) * s
    gain = lambda k, shape: 1.0 + 0.05 * jax.random.normal(k, shape, jnp.float32)
    a_init = jax.random.uniform(ks[19], (N_EVEN, D_B), jnp.float32, 0.9, 0.999)
    return {
        'x_prompt': nrm(ks[0], (BATCH, SEQ, D_MODEL), 1.0),
        'x_sample': nrm(ks[1], (DEC_BATCH, DEC_SEQ, D_MODEL), 1.0),
        'cache_b_conv': nrm(ks[2], (N_EVEN, DEC_BATCH, B_CONV - 1, D_B), 1.0),
        'state_b_h': nrm(ks[3], (N_EVEN, DEC_BATCH, D_B), 0.5),
        'cache_c_conv': nrm(ks[4], (N_ODD, DEC_BATCH, C_CONV - 1, D_C), 1.0),
        'norm_mix_pre': gain(ks[5], (DEPTH, D_MODEL)),
        'norm_mix_post': gain(ks[6], (DEPTH, D_MODEL)),
        'norm_ffn_pre': gain(ks[7], (DEPTH, D_MODEL)),
        'norm_ffn_post': gain(ks[8], (DEPTH, D_MODEL)),
        'w_in_even': nrm(ks[9], (N_EVEN, D_MODEL, D_IN_EVEN), D_MODEL ** -0.5),
        'a_v_gain': gain(ks[10], (N_EVEN, D_A)),
        'a_w_s': nrm(ks[11], (N_EVEN, A_HEADS, A_CHUNK, A_CHUNK), A_CHUNK ** -0.5),
        'a_b_s': 1.0 + 0.1 * jax.random.normal(ks[12], (N_EVEN, A_HEADS, A_CHUNK), jnp.float32),
        'b_conv_w': nrm(ks[13], (N_EVEN, B_CONV, D_B), B_CONV ** -0.5),
        'b_conv_b': nrm(ks[14], (N_EVEN, D_B), 0.01),
        'b_wa': nrm(ks[15], (N_EVEN, B_HEADS, B_HEAD_DIM, B_HEAD_DIM), B_HEAD_DIM ** -0.5),
        'b_ba': nrm(ks[16], (N_EVEN, D_B), 0.1),
        'b_wx': nrm(ks[17], (N_EVEN, B_HEADS, B_HEAD_DIM, B_HEAD_DIM), B_HEAD_DIM ** -0.5),
        'b_bx': nrm(ks[18], (N_EVEN, D_B), 0.1),
        'b_lambda': jnp.log(a_init) - jnp.log1p(-a_init),
        'w_out_even': nrm(ks[20], (N_EVEN, D_A + D_B, D_MODEL), (D_A + D_B) ** -0.5),
        'c_w_in': nrm(ks[21], (N_ODD, D_MODEL, 3 * D_C), D_MODEL ** -0.5),
        'c_conv_w': nrm(ks[22], (N_ODD, C_CONV, D_C), C_CONV ** -0.5),
        'c_w_out': nrm(ks[23], (N_ODD, D_C, D_MODEL), D_C ** -0.5),
        'mlp_up': nrm(ks[24], (DEPTH, D_MODEL, D_FF), D_MODEL ** -0.5),
        'mlp_down': nrm(ks[25], (DEPTH, D_FF, D_MODEL), D_FF ** -0.5),
    }

def reference(x_prompt, x_sample, cache_b_conv, state_b_h, cache_c_conv,
              norm_mix_pre, norm_mix_post, norm_ffn_pre, norm_ffn_post,
              w_in_even, a_v_gain, a_w_s, a_b_s, b_conv_w, b_conv_b, b_wa, b_ba, b_wx, b_bx,
              b_lambda, w_out_even, c_w_in, c_conv_w, c_w_out, mlp_up, mlp_down):
    p = dict(norm_mix_pre=norm_mix_pre, norm_mix_post=norm_mix_post,
             norm_ffn_pre=norm_ffn_pre, norm_ffn_post=norm_ffn_post,
             w_in_even=w_in_even, a_v_gain=a_v_gain, a_w_s=a_w_s, a_b_s=a_b_s,
             b_conv_w=b_conv_w, b_conv_b=b_conv_b, b_wa=b_wa, b_ba=b_ba, b_wx=b_wx, b_bx=b_bx,
             b_lambda=b_lambda, w_out_even=w_out_even, c_w_in=c_w_in, c_conv_w=c_conv_w,
             c_w_out=c_w_out, mlp_up=mlp_up, mlp_down=mlp_down)
    dt = x_prompt.dtype
    zb = jnp.zeros((N_EVEN, BATCH, B_CONV - 1, D_B), dt)
    zh = jnp.zeros((N_EVEN, BATCH, D_B), dt)
    zc = jnp.zeros((N_ODD, BATCH, C_CONV - 1, D_C), dt)
    y_prompt, _, bconv_p, bh_p, cconv_p = trunk(x_prompt, zb, zh, zc, p)
    y_sample, v_s, bconv_s, bh_s, cconv_s = trunk(x_sample, cache_b_conv, state_b_h, cache_c_conv, p)
    return (y_prompt, y_sample, v_s, bconv_p, bh_p, cconv_p, bconv_s, bh_s, cconv_s)


_drawn_inputs = setup_inputs


def setup_inputs(seed=0):
    import zlib

    import numpy as np

    out = dict(_drawn_inputs(seed))
    spreads = {}
    factors = {}
    for name, (base, spread) in spreads.items():
        noise = np.random.default_rng([zlib.crc32(name.encode()), seed]).standard_normal(out[name].shape)
        drawn = base * np.exp(spread * noise) if base else spread * noise
        out[name] = __import__('jax').numpy.asarray(drawn.astype(out[name].dtype))
    for name, factor in factors.items():
        out[name] = (out[name] * factor).astype(out[name].dtype)
    return out
```

```python
from contextlib import ExitStack

import concourse.bass as bass
from concourse import mybir

P = 128
D = 1024
SEQ = 1024
DEC = 32
TOK = SEQ + DEC
NT = 3
TT = TOK // NT
KC = D // P
FF = 4096
GROUPS = FF // D
HALF = D // 2
HC = HALF // P
EPS = 1e-6
CB = 4
CC = 3
NJ = 4
JW = TT // NJ

EVEN_IN = 0
EVEN_OUT = EVEN_IN + 16
MLP = [EVEN_OUT + 8, 0]
ODD_IN = MLP[0] + 16 * GROUPS
ODD_OUT = ODD_IN + 24
MLP[1] = ODD_OUT + 8
PANELS = MLP[1] + 16 * GROUPS

LB = (CB - 1) + SEQ + (CB - 1) + DEC
LV = LB - (CB - 1)
LT = LV // 3
LS = SEQ + CB - 1
PB = (CC - 1) + SEQ + (CC - 1) + DEC
PV = PB - (CC - 1)
PS = SEQ + CC - 1

F32 = mybir.dt.float32
F32R = mybir.dt.float32r
ALU = mybir.AluOpType
ACT = mybir.ActivationFunctionType
ds = bass.ds


def tile_pieces(t):
    lo, hi = t * TT, (t + 1) * TT
    if hi <= SEQ:
        return [(0, TT, lo, False)]
    return [(0, SEQ - lo, lo, False), (SEQ - lo, hi - SEQ, SEQ, True)]


def build(nc, A, O):
    with ExitStack() as ctx:
        at_byte = [nc.sbuf_base + (-nc.sbuf_base) % 32]

        def place(name, shape, dt, offset=None):
            size = 4
            for n in shape[1:]:
                size *= n
            here = at_byte[0] if offset is None else offset
            if offset is None:
                at_byte[0] += size + (-size) % 32
            return nc.alloc_sbuf_tensor_at(name, shape, dt, offset=here)

        def sem(name):
            return ctx.enter_context(nc.semaphore(name))

        CH = KC * TOK
        x_hi = place("x_hi", [P, CH], F32R)
        at_x_lo = at_byte[0]
        x_lo = place("x_lo", [P, CH], F32R)
        x_sum = place("x_sum", [P, CH], F32, at_x_lo)
        at_h_hi = at_byte[0]
        h_hi = place("h_hi", [P, CH], F32R)
        at_h_lo = at_byte[0]
        h_lo = place("h_lo", [P, CH], F32R)
        at_f = at_byte[0]
        f = place("f", [P, CH], F32)
        w_raw = [place(f"w_raw{s}", [P, D], F32) for s in range(2)]
        w_hi = [place(f"w_hi{s}", [P, D], F32R) for s in range(2)]
        w_lo = [place(f"w_lo{s}", [P, D], F32R) for s in range(2)]
        sq_sum = place("sq_sum", [P, TOK], F32)
        rstd = place("rstd", [P, TOK], F32)
        tmp = [place(f"tmp{t}", [P, TT], F32) for t in range(NT)]
        ident = place("ident", [P, P], F32)
        ones = place("ones", [P, P], F32)
        eps = place("eps", [P, 1], F32)
        root = place("root", [P, NJ], F32)
        rcol = place("rcol", [P, NJ], F32)
        gains = place("gains", [P, 8, KC], F32)
        b_conv_w = place("b_conv_w", [P, CB, HC], F32)
        b_vec = place("b_vec", [P, 4, HC], F32)
        soft = place("soft", [P, 8, HC], F32)
        c_conv_w = place("c_conv_w", [P, CC, KC], F32)
        b_tail = place("b_tail", [P, 2, HC, CB - 1], F32)
        h_tail = place("h_tail", [P, 2, HC], F32)
        h_init = place("h_init", [P, HC], F32)
        c_tail = place("c_tail", [P, 2, KC, CC - 1], F32)
        v_sq = place("v_sq", [P, 9], F32)
        v_root = place("v_root", [P, 9], F32)
        v_rstd = place("v_rstd", [P, 9], F32)

        x_rows = place("x_rows", [P, SEQ // P, D], F32, at_h_hi)
        x_rows_s = place("x_rows_s", [DEC, D], F32, at_h_lo)
        gate_w = place("gate_w", [P, 2, HC, P], F32, at_h_hi)
        xb_pad = place("xb_pad", [P, HC, LB], F32, at_h_hi + 3 * TOK * 4)
        v_tok = place("v_tok", [P, SEQ // P, HALF], F32, at_h_lo)
        hr = place("hr", [P, HC, TOK], F32, at_h_lo + HC * TOK * 4)
        lru_step = LV * 4 + (-LV * 4) % 32
        lru = [place(f"lru{i}", [P, LV], F32, at_f + i * lru_step) for i in range(4)]
        spatial = place("spatial", [P, HC, TOK], F32, at_f)
        o = at_f + 4 * lru_step
        gelu = [place(f"gelu{i}", [P, TOK], F32, o + i * TOK * 4) for i in range(2)]
        ws_raw = place("ws_raw", [P, HC, P], F32, o + TOK * 4)
        o += 2 * TOK * 4
        bias_bc = place("bias_bc", [P, HC, P], F32, o)
        v_tok_s = place("v_tok_s", [DEC, HALF], F32, o + HALF * 4)
        ws_t = place("ws_t", [P, HC, P], F32, o + 2 * HALF * 4)
        v_gain_bc = place("v_gain_bc", [P, HALF], F32, o + 3 * HALF * 4)
        assert o + 4 * HALF * 4 <= at_f + CH * 4
        cg = [place(f"cg{i}", [P, TOK], F32, at_f + i * TOK * 4) for i in range(2)]
        c_step = PB * 4 + (-PB * 4) % 32
        cp = [place(f"cp{i}", [P, PB], F32, at_f + 2 * TOK * 4 + i * c_step) for i in range(2)]
        cy = [place(f"cy{i}", [P, PV], F32, at_f + 2 * TOK * 4 + (2 + i) * c_step) for i in range(2)]
        y_rows = place("y_rows", [P, SEQ // P, D], F32, at_h_hi)
        y_rows_s = place("y_rows_s", [DEC, D], F32, at_h_lo)

        ps = ctx.enter_context(nc.psum_tensor("ps", [P, 8, 512], F32))
        M0, M1 = 6, 7

        w_in = [sem(f"w_in{s}") for s in range(2)]
        w_gained = sem("w_gained")
        w_high = sem("w_high")
        w_ready = sem("w_ready")
        pe_tile = sem("pe_tile")
        evac = sem("evac")
        x_in = sem("x_in")
        c_in = sem("c_in")
        s_in = sem("s_in")
        b_in = sem("b_in")
        g_in = sem("g_in")
        pad_in = sem("pad_in")
        cpad_in = sem("cpad_in")
        consts = sem("consts")
        zeros = sem("zeros")
        czeros = sem("czeros")
        soft_ok = sem("soft_ok")
        soft_act = sem("soft_act")
        x0_t = sem("x0_t")
        x0_a = sem("x0_a")
        x0_b = sem("x0_b")
        col = sem("col")
        rooted = sem("rooted")
        inverted = sem("inverted")
        diag = sem("diag")
        bc = sem("bc")
        rs_ready = sem("rs_ready")
        f_sq = sem("f_sq")
        f_acc = sem("f_acc")
        xs = sem("xs")
        upd_a = sem("upd_a")
        upd_x = sem("upd_x")
        upd_act = sem("upd_act")
        x_ready = sem("x_ready")
        upd_acc = sem("upd_acc")
        h_sq = sem("h_sq")
        h_high = sem("h_high")
        h_ready = sem("h_ready")
        conv = sem("conv")
        gate_pe = sem("gate_pe")
        gate_act = sem("gate_act")
        lru_act = sem("lru_act")
        lru_dve = sem("lru_dve")
        lru_pool = sem("lru_pool")
        scanned = sem("scanned")
        tails = sem("tails")
        gelued = sem("gelued")
        ws_pe = sem("ws_pe")
        ws_ok = sem("ws_ok")
        ws_masked = sem("ws_masked")
        vt_pe = sem("vt_pe")
        vt_ok = sem("vt_ok")
        v_ss = sem("v_ss")
        v_rt = sem("v_rt")
        v_inv = sem("v_inv")
        v_ok = sem("v_ok")
        sgu_pe = sem("sgu_pe")
        sgu_ok = sem("sgu_ok")
        mix_mul = sem("mix_mul")
        mix_high = sem("mix_high")
        mix_ready = sem("mix_ready")
        cp_ok = sem("cp_ok")
        cconv = sem("cconv")
        ctails = sem("ctails")
        y_pe = sem("y_pe")
        y_a = sem("y_a")
        y_b = sem("y_b")
        out_dma = sem("out_dma")

        MIX_G, MIX_PRE_N = 0, 0
        G_MIX_PRE, G_FFN_PRE, G_MIX_POST, G_FFN_POST = 0, 2, 4, 6

        def pt(buf, c, t):
            return buf[:, ds(c * TOK + t * TT, TT)]

        def bank(p2, t):
            return ps[:, p2 * NT + t, 0:TT]

        def wait(eng, s, n):
            if not isinstance(n, int) or n > 0:
                eng.wait_ge(s, n)

        def post_n(b, t):
            return 3 + 6 * b + t

        def pre_n(u, t):
            return 6 * u + t

        LAST = [EVEN_OUT + 7, MLP[0] + 63, ODD_OUT + 7, MLP[1] + 63]
        POST_GAIN = [G_MIX_POST, G_FFN_POST, G_MIX_POST + 1, G_FFN_POST + 1]

        EVEN_COLS = [8 + j for j in range(4)] + [4 + j for j in range(4)] + [12 + j for j in range(4)] + list(range(4))

        ctx.enter_context(nc.allow_non_contiguous_dma(reason="one value to a partition: a few KB in all"))
        block = ctx.enter_context(nc.Block())

        @block.sync
        def _(sp):
            def panel(p, src):
                wait(sp, w_ready, p - 1)
                sp.dma_start(w_raw[p % 2][:, :].rearrange("p (k n) -> p k n", k=KC), src).then_inc(w_in[p % 2], 16)

            def panel_at(p, s, src):
                sp.wait_ge(w_ready, p - 1)
                sp.dma_start(w_raw[s][:, :].rearrange("p (k n) -> p k n", k=KC), src).then_inc(w_in[s], 16)

            def rows(w, r0, c):
                return w[r0:r0 + D, ds(c * P, P)].rearrange("(k p) n -> p k n", p=P)

            xp = A["x_prompt"][0].rearrange("(n p) d -> p n d", p=P)
            for n in range(0, SEQ // P, 2):
                sp.dma_start(x_rows[:, n:n + 2, :], xp[:, n:n + 2, :]).then_inc(x_in, 16)
            sp.dma_start(x_rows_s[:, :], A["x_sample"][0]).then_inc(x_in, 16)
            w_even = A["w_in_even"][0]
            for p in range(2):
                panel(p, rows(w_even, 0, EVEN_COLS[p]))

            sp.wait_ge(zeros, 2)
            for g, name in ((0, "b_wa"), (1, "b_wx")):
                for half in range(2):
                    src = A[name][0].rearrange("(c two) i j -> two i c j", two=2)[half]
                    q = 64 * half
                    sp.dma_start(gate_w[q:q + 64, g, :, q:q + 64], src).then_inc(g_in, 16)
            for c in range(HC):
                sp.dma_start(xb_pad[:, c, LS:LS + CB - 1],
                             A["cache_b_conv"][0, 0][:, c * P:(c + 1) * P].rearrange("r p -> p r")).then_inc(pad_in, 16)
            sp.wait_ge(upd_acc, 21)
            sp.dma_start(ws_raw[:, :, :], A["a_w_s"][0].rearrange("h i j -> i h j")).then_inc(s_in, 16)
            sp.dma_start(v_gain_bc[:, :], A["a_v_gain"].to_broadcast([P, HALF])).then_inc(s_in, 16)
            sp.dma_start(bias_bc[:, :, :], A["a_b_s"][0:1].to_broadcast([P, HC, P])).then_inc(b_in, 16)

            for p in range(2, 16):
                panel(p, rows(w_even, 0, EVEN_COLS[p]))
            sp.wait_ge(v_ok, 9)
            sp.dma_start(O["v"][0, 0], v_tok_s[:, :]).then_inc(out_dma, 16)
            sp.wait_ge(tails, 3 * HC)
            for i, name in ((0, "bconv_p"), (1, "bconv_s")):
                for c in range(HC):
                    sp.dma_start(O[name][0, 0][:, c * P:(c + 1) * P].rearrange("r p -> p r"),
                                 b_tail[:, i, c, :]).then_inc(out_dma, 16)
            for i, name in ((0, "bh_p"), (1, "bh_s")):
                sp.dma_start(O[name][0, 0].rearrange("(c p) -> p c", p=P), h_tail[:, i, :]).then_inc(out_dma, 16)

            def pairs(base, n, w, r0, c0=0):
                with sp.Fori(0, n // 2) as i:
                    for s in range(2):
                        panel_at(base + 2 * i + s, s, rows(w, r0, c0 + 2 * i + s))

            def mlp_loads(l):
                up, down = A["mlp_up"][l], A["mlp_down"][l]
                for g in range(GROUPS):
                    pairs(MLP[l] + 16 * g, 8, up, 0, 8 * g)
                    pairs(MLP[l] + 16 * g + 8, 8, down, g * D)

            pairs(EVEN_OUT, 8, A["w_out_even"][0], 0)
            mlp_loads(0)
            w_odd = A["c_w_in"][0]

            def odd_loads(i):
                for q in range(6):
                    c = 2 * i + q // 3
                    part = (1, 2, 0)[q % 3]
                    panel_at(ODD_IN + 6 * i + q, q % 2, rows(w_odd, 0, part * KC + c))
                    if q % 3 == 1:
                        sp.wait_ge(czeros, 2)
                        wait(sp, cconv, 3 * c - 3)
                        sp.dma_start(cp[q // 3][:, PS:PS + CC - 1],
                                     A["cache_c_conv"][0, 0][:, ds(c * P, P)].rearrange("r p -> p r")
                                     ).then_inc(cpad_in, 16)

            odd_loads(0)
            with sp.Fori(1, KC // 2) as i:
                odd_loads(i)
            sp.wait_ge(ctails, 2 * KC)
            for i, name in ((0, "cconv_p"), (1, "cconv_s")):
                for c in range(KC):
                    sp.dma_start(O[name][0, 0][:, c * P:(c + 1) * P].rearrange("r p -> p r"),
                                 c_tail[:, i, c, :]).then_inc(out_dma, 16)
            pairs(ODD_OUT, 8, A["c_w_out"][0], 0)
            mlp_loads(1)
            yp = O["y_prompt"][0].rearrange("(n p) d -> p n d", p=P)
            for n in range(SEQ // P):
                sp.wait_ge(y_a, n + 1)
                sp.wait_ge(y_b, n + 1)
                sp.dma_start(yp[:, n, :], y_rows[:, n, :]).then_inc(out_dma, 16)
            sp.wait_ge(y_a, 9)
            sp.wait_ge(y_b, 9)
            sp.dma_start(O["y_sample"][0], y_rows_s[:, :]).then_inc(out_dma, 16)
            sp.wait_ge(out_dma, 16 * (1 + 2 * HC + 2 + 2 * KC + SEQ // P + 1))

        @block.gpsimd
        def _(pool):
            nc.gpsimd.memset(ones[:, :], 1.0).then_inc(consts, 1)
            nc.gpsimd.memset(ident[:, :], 0.0).then_inc(consts, 1)
            nc.gpsimd.memset(eps[:, :], EPS).then_inc(consts, 1)
            pool.wait_ge(consts, 3)
            nc.gpsimd.affine_select(out=ident[:, :], in_=ident[:, :], compare_op=ALU.not_equal, fill=1.0, base=0,
                                    pattern=[[-1, P]], channel_multiplier=1).then_inc(consts, 1)

            def split(p, s, load, gain=None, gained=None):
                pool.wait_ge(w_in[s], 16 * load)
                if gain is not None:
                    raw = w_raw[s][:, :].rearrange("p (k n) -> p k n", k=KC)
                    nc.gpsimd.tensor_tensor(raw, raw, gains[:, gain, :].unsqueeze(2).to_broadcast([P, KC, P]),
                                            ALU.mult).then_inc(w_gained, 1)
                    pool.wait_ge(w_gained, gained + 1)
                wait(pool, pe_tile, 3 * p - 3)
                nc.gpsimd.tensor_tensor(w_hi[s][:, :], w_raw[s][:, :], ones[:, 0:1].to_broadcast([P, D]),
                                        ALU.mult).then_inc(w_high, 1)
                pool.wait_ge(w_high, p + 1)
                nc.gpsimd.tensor_tensor(w_lo[s][:, :], w_raw[s][:, :], w_hi[s][:, :].bitcast(F32),
                                        ALU.subtract).then_inc(w_ready, 1)

            def x_low(u, t, k):
                n = 24 * u + 8 * t + k
                pool.wait_ge(upd_act, 2 * (n + 1))
                nc.gpsimd.tensor_tensor(pt(x_lo, k, t), pt(x_sum, k, t), pt(x_hi, k, t).bitcast(F32),
                                        ALU.subtract).then_inc(x_ready, 1)

            def join_x(b, after):
                pool.wait_ge(pe_tile, 3 * after)
                for k in range(KC):
                    nc.gpsimd.tensor_tensor(x_sum[:, k * TOK:(k + 1) * TOK], x_hi[:, k * TOK:(k + 1) * TOK].bitcast(F32),
                                            x_lo[:, k * TOK:(k + 1) * TOK].bitcast(F32), ALU.add).then_inc(xs, 1)

            def update(b):
                for t in range(NT):
                    for k in range(KC + 2):
                        if k < KC:
                            pool.wait_ge(upd_a, 24 * b + 8 * t + k + 1)
                            pool.wait_ge(xs, 8 * b + k + 1)
                            nc.gpsimd.tensor_tensor(pt(x_sum, k, t), pt(x_sum, k, t), pt(f, k, t),
                                                    ALU.add).then_inc(upd_x, 1)
                        if k >= 2 and b < 3:
                            x_low(b + 1, t, k - 2)

            pool.wait_ge(consts, 4)
            pool.wait_ge(c_in, 16 * N_VEC)
            split(0, 0, 1, G_MIX_PRE, 0)
            split(1, 1, 1, G_MIX_PRE, 1)
            pool.wait_ge(x0_t, 9)
            nc.gpsimd.memset(gate_w[:, :, :, :], 0.0).then_inc(zeros, 1)
            nc.gpsimd.memset(xb_pad[:, :, 0:CB - 1], 0.0).then_inc(zeros, 1)
            for t in range(NT):
                for k in range(KC):
                    x_low(0, t, k)

            mixed = 0

            def mix_product(base, buf, hidden, c, t):
                pass

            for p in range(16):
                if p > 0:
                    split(p + 1, (p + 1) % 2, (p + 1) // 2 + 1, G_MIX_PRE if p + 1 < 16 else None, p + 1)
                if p == 0:
                    pool.wait_ge(ws_ok, 1)
                    nc.gpsimd.memset(ws_t[64:P, :, 0:64], 0.0).then_inc(ws_masked, 1)
                    pool.wait_ge(ws_masked, 1)
                if p % 2 == 1 and p < 8:
                    j = p // 2
                    xc, q, ig, rc = lru
                    pool.wait_ge(gate_act, 6 * j + 6)
                    nc.gpsimd.tensor_tensor(ig[:, :], ig[:, :], xc[:, :], ALU.mult).then_inc(lru_pool, 1)
                    pool.wait_ge(lru_act, 2 * j + 2)
                    pool.wait_ge(lru_dve, 3 * j + 2)
                    nc.gpsimd.tensor_tensor(q[:, :], q[:, :], rc[:, :], ALU.mult).then_inc(lru_pool, 1)
                    pool.wait_ge(lru_pool, 3 * j + 2)
                    nc.gpsimd.tensor_tensor(q[:, :], q[:, :], ig[:, :], ALU.mult).then_inc(lru_pool, 1)
                if p >= 8:
                    c = p - 8
                    buf, m = (hr, c) if c < 4 else (spatial, c - 4)
                    ch = 4 + c if c < 4 else c - 4
                    for t in range(NT):
                        n = 3 * c + t
                        tile = buf[:, m, t * TT:(t + 1) * TT]
                        pool.wait_ge(gelued, 12 + n + 1)
                        if c < 4 and t == 0:
                            pool.wait_ge(scanned, 2 * c + 2)
                            pool.wait_ge(tails, 3 * c + 3)
                        if c >= 4 and t == 0:
                            pool.wait_ge(sgu_ok, 3 * (c - 4) + 3)
                        nc.gpsimd.tensor_tensor(tile, tile, gelu[p % 2][:, t * TT:(t + 1) * TT],
                                                ALU.mult).then_inc(mix_mul, 1)
                        pool.wait_ge(mix_mul, n + 1)
                        pool.wait_ge(mix_high, n + 1)
                        nc.gpsimd.tensor_tensor(pt(h_lo, ch, t), tile, pt(h_hi, ch, t).bitcast(F32),
                                                ALU.subtract).then_inc(mix_ready, 1)

            def out_phase(base, b, next_gain, next_gained):
                split(base + 1, 1, base // 2 + 1)
                join_x(b, base)
                with pool.Fori(0, 3) as i:
                    split(base + 2 + 2 * i, 0, base // 2 + 2 + i)
                    split(base + 3 + 2 * i, 1, base // 2 + 2 + i)
                split(base + 8, 0, base // 2 + 5, next_gain, next_gained)
                update(b)

            def up_splits(base, gain, gained):
                split(base + 1, 1, base // 2 + 1, gain, gained + 1)
                with pool.Fori(0, 3) as i:
                    split(base + 2 + 2 * i, 0, base // 2 + 2 + i, gain, gained + 2 + 2 * i)
                    split(base + 3 + 2 * i, 1, base // 2 + 2 + i, gain, gained + 3 + 2 * i)
                split(base + 8, 0, base // 2 + 5)

            def mlp(l, b, gained, next_gain, next_gained):
                for g in range(GROUPS):
                    base = MLP[l] + 16 * g
                    up_splits(base, G_FFN_PRE + l, gained + 8 * g)
                    d = base + 8
                    if g < GROUPS - 1:
                        split(d + 1, 1, d // 2 + 1)
                        with pool.Fori(0, 3) as i:
                            split(d + 2 + 2 * i, 0, d // 2 + 2 + i)
                            split(d + 3 + 2 * i, 1, d // 2 + 2 + i)
                        split(d + 8, 0, d // 2 + 5, G_FFN_PRE + l, gained + 8 * g + 8)
                    else:
                        split(d + 1, 1, d // 2 + 1)
                        join_x(b, d)
                        with pool.Fori(0, 3) as i:
                            split(d + 2 + 2 * i, 0, d // 2 + 2 + i)
                            split(d + 3 + 2 * i, 1, d // 2 + 2 + i)
                        if next_gain is not None:
                            split(d + 8, 0, d // 2 + 5, next_gain, next_gained)
                        update(b)

            out_phase(EVEN_OUT, 0, G_FFN_PRE, 16)
            mlp(0, 1, 16, G_MIX_PRE + 1, 48)
            pool.wait_ge(upd_acc, 3 * 21)
            for i in range(2):
                nc.gpsimd.memset(cp[i][:, 0:CC - 1], 0.0).then_inc(czeros, 1)

            def odd_pool(c, q):
                pass

            def odd_slot(p, s, load, gained, c, q, kind, more=True):
                if more:
                    split(p + 1, 1 - s, load, G_MIX_PRE + 1, gained)
                else:
                    split(p + 1, 1 - s, load)
                if kind == 1:
                    for t in range(NT):
                        pool.wait_ge(evac, 3 * p + t + 1)
                        for (o0, n, tok, smp) in tile_pieces(t):
                            dst = (PS + CC - 1) if smp else (CC - 1 + tok)
                            nc.gpsimd.tensor_tensor(cp[q][:, dst:dst + n], tmp[t][:, o0:o0 + n], cg[q][:, tok:tok + n],
                                                    ALU.mult).then_inc(cp_ok, 1)
                if kind == 2:
                    pool.wait_ge(cconv, 3 * c + 3)
                    for t in range(NT):
                        n0 = 4 * c + t
                        pool.wait_ge(evac, 3 * p + t + 1)
                        for j, (o0, n, tok, smp) in enumerate(tile_pieces(t)):
                            y = cy[q][:, (PS if smp else tok):(PS if smp else tok) + n]
                            nc.gpsimd.tensor_tensor(y, tmp[t][:, o0:o0 + n], y, ALU.mult).then_inc(mix_mul, 1)
                            pool.wait_ge(mix_mul, 24 + n0 + j + 1)
                            pool.wait_ge(mix_high, 24 + n0 + j + 1)
                            lo = h_lo[:, ds(c * TOK + tok, n)]
                            hi = h_hi[:, ds(c * TOK + tok, n)]
                            nc.gpsimd.tensor_tensor(lo, y, hi.bitcast(F32), ALU.subtract).then_inc(mix_ready, 1)

            def odd_body(i, last):
                for q in range(6):
                    p = ODD_IN + 6 * i + q
                    load = (ODD_IN // 2) + 3 * i + (q + 1) // 2 + 1
                    odd_slot(p, q % 2, load, 48 + 6 * i + q + 1, 2 * i + q // 3, q // 3, q % 3,
                             more=not (last and q == 5))

            with pool.Fori(0, KC // 2 - 1) as i:
                odd_body(i, False)
            odd_body(KC // 2 - 1, True)
            out_phase(ODD_OUT, 2, G_FFN_PRE + 1, 72)
            mlp(1, 3, 72, None, None)

        @block.tensor
        def _(pe):
            def mm3(dst, s, src_hi, src_lo, t, k, hook=None):
                hi, lo = pt(src_hi, k, t), pt(src_lo, k, t)
                wh, wl = w_hi[s][:, k * P:(k + 1) * P], w_lo[s][:, k * P:(k + 1) * P]
                nc.tensor.matmul(dst, wh, hi, start=(k == 0), stop=False)
                nc.tensor.matmul(dst, wh, lo, start=False, stop=False)
                return nc.tensor.matmul(dst, wl, hi, start=False, stop=(k == KC - 1))

            def panel(p, s, src, before=None, mid=None, after=None):
                pe.wait_ge(w_ready, p + 1)
                for t in range(NT):
                    wait(pe, evac, 3 * p - 5 + t)
                    for k in range(KC):
                        if before:
                            before(t, k)
                        last = mm3(bank(s, t), s, src[0], src[1], t, k)
                        if k == KC - 1:
                            last.then_inc(pe_tile, 1)
                        if mid:
                            mid(t, k)
                    if after:
                        after(t)

            X, H = (x_hi, x_lo), (h_hi, h_lo)

            def col_sums(n, t, s, v):
                pe.wait_ge(s, v)
                wait(pe, rooted, n)
                for j in range(NJ):
                    c0 = t * TT + j * JW
                    last = nc.tensor.matmul(ps[0:JW, M0, j:j + 1], sq_sum[:, c0:c0 + JW], ones[:, 0:1],
                                            start=True, stop=True)
                last.then_inc(col, 1)

            def spread(n, t):
                pe.wait_ge(diag, n + 1)
                wait(pe, rs_ready, n)
                nc.tensor.matmul(ps[:, M1, 0:TT], ones[0:JW, :], tmp[t][0:JW, :], start=True, stop=True).then_inc(bc, 1)

            def first_two(base, u, after_panel=None):
                def before(t, k):
                    pe.wait_ge(x_ready, 24 * u + 8 * t + k + 1)

                def after0(t):
                    if t > 0:
                        spread(pre_n(u, t - 1), t - 1)
                    col_sums(pre_n(u, t), t, upd_acc, 21 * u + 7 * t + 7)

                def after1(t):
                    if t == 0:
                        spread(pre_n(u, NT - 1), NT - 1)

                panel(base, 0, X, before=before, after=after0)
                if after_panel:
                    after_panel(0)
                panel(base + 1, 1, X, after=after1)

            def pairs(base, n, src, before=None):
                with pe.Fori(0, n) as i:
                    for s in range(2):
                        panel(base + 2 * i + s, s, src, before=before if s == 0 else None)

            def last_panel(b):
                def mid(t, k):
                    if t == 2 and k == 4:
                        spread(post_n(b, 0), 0)

                def after(t):
                    if t == 1:
                        col_sums(post_n(b, 0), 0, f_acc, 24 * b + 21 + 1)
                    if t == 2:
                        col_sums(post_n(b, 1), 1, f_acc, 24 * b + 21 + 2)
                        col_sums(post_n(b, 2), 2, f_acc, 24 * b + 21 + 3)
                        spread(post_n(b, 1), 1)
                        spread(post_n(b, 2), 2)

                panel(LAST[b], 1, H, mid=mid, after=after)

            def mlp(l, u):
                for g in range(GROUPS):
                    base = MLP[l] + 16 * g
                    if g == 0:
                        first_two(base, u)
                        pairs(base + 2, 3, X)
                    else:
                        pairs(base, 4, X)
                    done = 96 * l + 24 * g

                    def before(t, k, done=done):
                        if k == 0 and t == 0:
                            pe.wait_ge(h_ready, done + 21)
                        if k == KC - 1:
                            pe.wait_ge(h_ready, done + 21 + t + 1)
                    if g < GROUPS - 1:
                        pairs(base + 8, 4, H, before)
                    else:
                        pairs(base + 8, 3, H, before)
                        panel(base + 14, 0, H)
                        last_panel(2 * l + 1)

            pe.wait_ge(consts, 4)
            pe.wait_ge(x_in, 16 * 5)
            for k in range(KC):
                a = 2 * (k % 3)
                wait(pe, x0_a, k - 2)
                wait(pe, x0_b, k - 2)
                for n in range(SEQ // P):
                    last = nc.tensor.transpose(ps[:, a + n // 4, (n % 4) * P:(n % 4 + 1) * P],
                                               x_rows[:, n, k * P:(k + 1) * P], ident[:, :])
                last.then_inc(x0_t, 1)
            for k in range(KC):
                last = nc.tensor.transpose(ps[:, M0, k * DEC:(k + 1) * DEC], x_rows_s[:, k * P:(k + 1) * P],
                                           ident[0:DEC, 0:DEC])
            last.then_inc(x0_t, 1)
            pe.wait_ge(x0_a, KC + 1)
            pe.wait_ge(x0_b, KC)

            def spatial_weights(_):
                pass

            def even_after(p):
                if p == 1:
                    pe.wait_ge(s_in, 32)
                    pe.wait_ge(rs_ready, 3)
                    for h in range(HC):
                        last = nc.tensor.transpose(ps[:, M1, h * P:(h + 1) * P], ws_raw[:, h, :], ident[:, :])
                    last.then_inc(ws_pe, 1)
                if p % 2 == 1 and p < 8:
                    j = p // 2
                    if j == 0:
                        pe.wait_ge(g_in, 64)
                        pe.wait_ge(ws_ok, 1)
                    pe.wait_ge(conv, 4 * j + 4)
                    for g in range(2):
                        for t in range(3):
                            n = 6 * j + 3 * g + t
                            wait(pe, gate_act, n - 1)
                            if j >= 3 and g == 0 and t == 0:
                                pe.wait_ge(vt_ok, 3 * (p - 5))
                            nc.tensor.matmul(ps[:, M0 + n % 2, 0:LT], gate_w[:, g, j, :],
                                             lru[0][:, t * LT:(t + 1) * LT], start=True, stop=True).then_inc(gate_pe, 1)
                if 5 <= p < 9:
                    c = p - 5
                    g = gelu[(4 + c) % 2]
                    pe.wait_ge(gate_act, 6 * min(4, (p + 1) // 2))
                    wait(pe, vt_ok, 3 * c)
                    pe.wait_ge(gelued, 3 * c + 3)
                    for half in range(2):
                        for n in range(4):
                            m = 4 * half + n
                            last = nc.tensor.transpose(ps[:, M0 + half, n * P:(n + 1) * P],
                                                       g[:, m * P:(m + 1) * P], ident[:, :])
                        last.then_inc(vt_pe, 1)
                    pe.wait_ge(vt_ok, 3 * c + 1)
                    nc.tensor.transpose(ps[0:DEC, M0, 0:P], g[:, SEQ:TOK], ident[:, :]).then_inc(vt_pe, 1)
                if p == 10:
                    pe.wait_ge(v_ok, 9)
                    pe.wait_ge(ws_masked, 1)
                    for h in range(HC):
                        for part in range(3):
                            n = 3 * h + part
                            wait(pe, sgu_ok, n - 1)
                            b = M0 + n % 2
                            if part < 2:
                                for q in range(4):
                                    m = 4 * part + q
                                    last = nc.tensor.matmul(ps[:, b, q * P:(q + 1) * P], v_tok[:, m, h * P:(h + 1) * P],
                                                            ws_t[:, h, :], start=True, stop=True)
                            else:
                                last = nc.tensor.matmul(ps[:, b, 0:DEC], v_tok_s[:, h * P:(h + 1) * P],
                                                        ws_t[0:DEC, h, 0:DEC], start=True, stop=True)
                            last.then_inc(sgu_pe, 1)

            first_two(EVEN_IN, 0)
            even_after(1)
            for p in range(2, 16):
                panel(p, p % 2, X)
                even_after(p)

            def before_even(t, k):
                if k == 0 and t == 0:
                    pe.wait_ge(mix_ready, 21)
                if k == HC - 1:
                    pe.wait_ge(mix_ready, 21 + t + 1)

            panel(EVEN_OUT, 0, H, before=before_even)
            panel(EVEN_OUT + 1, 1, H)
            pairs(EVEN_OUT + 2, 2, H)
            panel(EVEN_OUT + 6, 0, H)
            last_panel(0)
            mlp(0, 1)

            first_two(ODD_IN, 2)
            pairs(ODD_IN + 2, 11, X)

            def before_odd(t, k):
                if k == 0 and t == 0:
                    pe.wait_ge(mix_ready, 24 + 28)
                if k == KC - 1:
                    pe.wait_ge(mix_ready, 24 + 28 + (1, 2, 4)[t])

            panel(ODD_OUT, 0, H, before=before_odd)
            panel(ODD_OUT + 1, 1, H)
            pairs(ODD_OUT + 2, 2, H)
            panel(ODD_OUT + 6, 0, H)
            last_panel(2)
            mlp(1, 3)

            pe.wait_ge(evac, 3 * PANELS)
            for n in range(9):
                w = P if n < 8 else DEC
                t_end = (n * P + w - 1) // TT
                pe.wait_ge(upd_x, 24 * 3 + 8 * t_end + 8)
                wait(pe, y_a, n - 2)
                wait(pe, y_b, n - 2)
                for k in range(KC):
                    last = nc.tensor.transpose(ps[0:w, 2 * (n % 3) + k // 4, (k % 4) * P:(k % 4 + 1) * P],
                                               x_sum[:, k * TOK + n * P:k * TOK + n * P + w], ident[:, :])
                    if k % 4 == 3:
                        last.then_inc(y_pe, 1)

        @block.scalar
        def _(act):
            for i, (name, l) in enumerate([("norm_mix_pre", 0), ("norm_mix_pre", 1), ("norm_ffn_pre", 0),
                                           ("norm_ffn_pre", 1), ("norm_mix_post", 0), ("norm_mix_post", 1),
                                           ("norm_ffn_post", 0), ("norm_ffn_post", 1)]):
                act.dma_start(gains[:, i, :], A[name][l].rearrange("(k p) -> p k", p=P)).then_inc(c_in, 16)
            for i, name in enumerate(["b_conv_b", "b_ba", "b_bx", "b_lambda"]):
                act.dma_start(b_vec[:, i, :], A[name][0].rearrange("(k p) -> p k", p=P)).then_inc(c_in, 16)
            act.dma_start(h_init[:, :], A["state_b_h"][0, 0].rearrange("(k p) -> p k", p=P)).then_inc(c_in, 16)
            for i in range(CB):
                act.dma_start(b_conv_w[:, i, :], A["b_conv_w"][0, i].rearrange("(k p) -> p k", p=P)).then_inc(c_in, 16)
            for i in range(CC):
                act.dma_start(c_conv_w[:, i, :], A["c_conv_w"][0, i].rearrange("(k p) -> p k", p=P)).then_inc(c_in, 16)

            act.wait_ge(c_in, 16 * N_VEC)
            nc.scalar.activation(soft[:, 0, :], b_vec[:, 3, :], ACT.Abs).then_inc(soft_act, 1)
            act.wait_ge(soft_act, 1)
            nc.scalar.activation(soft[:, 1, :], soft[:, 0, :], ACT.Exp, scale=-1.0).then_inc(soft_act, 1)

            def rs_root(n):
                act.wait_ge(col, n + 1)
                act.wait_ge(consts, 4)
                wait(act, inverted, n)
                nc.scalar.activation(root[0:JW, :], ps[0:JW, M0, 0:NJ], ACT.Sqrt, bias=eps[0:JW, 0:1],
                                     scale=1.0 / D).then_inc(rooted, 1)

            def rs_copy(n, t):
                act.wait_ge(bc, n + 1)
                nc.scalar.copy(rstd[:, t * TT:(t + 1) * TT], ps[:, M1, 0:TT]).then_inc(rs_ready, 1)

            def split_x(u, t, k):
                if u > 0:
                    act.wait_ge(upd_x, 24 * (u - 1) + 8 * t + k + 1)
                nc.scalar.copy(pt(x_hi, k, t), pt(x_sum, k, t)).then_inc(upd_act, 1)
                nc.scalar.activation(pt(f, k, t), pt(x_sum, k, t), ACT.Square).then_inc(upd_act, 1)

            def square_out(b, p, m, t):
                n = 24 * b + 3 * m + t
                act.wait_ge(evac, 3 * p + t + 1)
                wait(act, f_acc, n - 2)
                nc.scalar.activation(tmp[t][:, :], pt(f, m, t), ACT.Square).then_inc(f_sq, 1)

            def first_pre(u):
                for t in range(NT):
                    rs_root(pre_n(u, t))
                    rs_copy(pre_n(u, t), t)

            def end_phase(b):
                p = LAST[b]
                square_out(b, p, 7, 0)
                square_out(b, p, 7, 1)
                rs_root(post_n(b, 0))
                rs_copy(post_n(b, 0), 0)
                square_out(b, p, 7, 2)
                rs_root(post_n(b, 1))
                rs_root(post_n(b, 2))
                rs_copy(post_n(b, 1), 1)
                rs_copy(post_n(b, 2), 2)
                if b < 3:
                    for t in range(NT):
                        for k in range(KC):
                            split_x(b + 1, t, k)

            def out_squares(b, base):
                for t in range(NT):
                    square_out(b, base, 0, t)
                with act.Fori(1, 7) as m:
                    for t in range(NT):
                        square_out(b, base + m, m, t)

            def mlp_up(n0, p, c, first=None):
                for t in range(NT):
                    if first is not None:
                        rs_root(pre_n(first, t))
                        rs_copy(pre_n(first, t), t)
                    act.wait_ge(evac, 3 * p + t + 1)
                    nc.scalar.activation(tmp[t][:, :], tmp[t][:, :], ACT.Square).then_inc(h_sq, 1)
                    act.wait_ge(h_sq, n0 + t + 1)
                    nc.scalar.copy(pt(h_hi, c, t), tmp[t][:, :]).then_inc(h_high, 1)

            def mlp(l, u):
                for g in range(GROUPS):
                    base = MLP[l] + 16 * g
                    if g == 0:
                        mlp_up(96 * l, base, 0, u)
                        with act.Fori(1, 8) as c:
                            mlp_up(96 * l + 3 * c, base + c, c)
                    else:
                        with act.Fori(0, 8) as c:
                            mlp_up(96 * l + 24 * g + 3 * c, base + c, c)
                out_squares(2 * l + 1, MLP[l] + 56)
                end_phase(2 * l + 1)

            for k in range(KC):
                act.wait_ge(x0_t, k + 1)
                nc.scalar.copy(x_sum[:, k * TOK + 512:k * TOK + SEQ], ps[:, 2 * (k % 3) + 1, :]).then_inc(x0_b, 1)
            act.wait_ge(x0_a, KC + 1)
            act.wait_ge(x0_b, KC)
            for t in range(NT):
                for k in range(KC):
                    split_x(0, t, k)
            first_pre(0)

            xc, q, ig, rc = lru
            for p in range(16):
                if p >= 1 and p < 8 and p % 2 == 0 or p == 8:
                    pass
                if p < 4:
                    act.wait_ge(evac, 3 * p + 3)
                    nc.scalar.copy(b_tail[:, 0, p, :], xb_pad[:, p, SEQ:SEQ + CB - 1]).then_inc(tails, 1)
                    nc.scalar.copy(b_tail[:, 1, p, :], xb_pad[:, p, LB - (CB - 1):LB]).then_inc(tails, 1)
                if p == 1:
                    act.wait_ge(ws_pe, 1)
                    nc.scalar.copy(ws_t[:, :, :].rearrange("p h j -> p (h j)"), ps[:, M1, :]).then_inc(ws_ok, 1)
                if p >= 4:
                    for t in range(NT):
                        n = 3 * (p - 4) + t
                        act.wait_ge(evac, 3 * p + t + 1)
                        if 6 <= p < 10:
                            act.wait_ge(vt_pe, 3 * (p - 5))
                        if p >= 10:
                            act.wait_ge(mix_mul, 3 * (p - 9))
                        if p == 5 and t == 0:
                            act.wait_ge(ws_pe, 1)
                        nc.scalar.activation(gelu[p % 2][:, t * TT:(t + 1) * TT], tmp[t][:, :],
                                             ACT.Gelu_apprx_tanh).then_inc(gelued, 1)
                        if p >= 8:
                            c = p - 8
                            buf, m = (hr, c) if c < 4 else (spatial, c - 4)
                            ch = 4 + c if c < 4 else c - 4
                            act.wait_ge(mix_mul, 3 * c + t + 1)
                            nc.scalar.copy(pt(h_hi, ch, t), buf[:, m, t * TT:(t + 1) * TT]).then_inc(mix_high, 1)
                if p % 2 == 1 and p < 8:
                    j = p // 2
                    for g in range(2):
                        for t in range(3):
                            n = 6 * j + 3 * g + t
                            act.wait_ge(gate_pe, n + 1)
                            if g == 0 and t == 0 and j > 0:
                                act.wait_ge(scanned, 2 * j)
                            dst = (q, ig)[g]
                            nc.scalar.activation(dst[:, t * LT:(t + 1) * LT], ps[:, M0 + n % 2, 0:LT], ACT.Sigmoid,
                                                 bias=b_vec[:, 1 + g, j:j + 1]).then_inc(gate_act, 1)
                    act.wait_ge(gate_act, 6 * j + 3)
                    if j == 0:
                        act.wait_ge(soft_ok, SOFT_STEPS)
                    nc.scalar.activation(q[:, :], q[:, :], ACT.Tanh, scale=soft[:, 7, j:j + 1]).then_inc(lru_act, 1)
                    act.wait_ge(lru_act, 2 * j + 1)
                    act.wait_ge(lru_dve, 3 * j + 1)
                    nc.scalar.activation(q[:, :], q[:, :], ACT.Sqrt, scale=4.0).then_inc(lru_act, 1)
                if 5 <= p < 9:
                    c = p - 5
                    for half in range(2):
                        act.wait_ge(vt_pe, 3 * c + half + 1)
                        nc.scalar.copy(v_tok[:, 4 * half:4 * half + 4, c * P:(c + 1) * P],
                                       ps[:, M0 + half, :].rearrange("p (n j) -> p n j", n=4)).then_inc(vt_ok, 1)
                    act.wait_ge(vt_pe, 3 * c + 3)
                    nc.scalar.copy(v_tok_s[:, c * P:(c + 1) * P], ps[0:DEC, M0, 0:P]).then_inc(vt_ok, 1)
                if p in (2, 4, 6, 8):
                    j = p // 2 - 1
                    act.wait_ge(scanned, 2 * j + 2)
                    nc.scalar.copy(h_tail[:, 0, j:j + 1], hr[:, j, SEQ - 1:SEQ]).then_inc(tails, 1)
                    nc.scalar.copy(h_tail[:, 1, j:j + 1], hr[:, j, TOK - 1:TOK]).then_inc(tails, 1)
                if p == 8:
                    act.wait_ge(vt_ok, 12)
                    act.wait_ge(lru_act, 8)
                    act.wait_ge(scanned, 8)
                    for n in range(8):
                        nc.scalar.activation(lru[1][:, 0:HALF], v_tok[:, n, :], ACT.Square,
                                             accum_out=v_sq[:, n:n + 1]).then_inc(v_ss, 1)
                        act.wait_ge(v_ss, n + 1)
                    nc.scalar.activation(lru[1][0:DEC, 0:HALF], v_tok_s[:, :], ACT.Square,
                                         accum_out=v_sq[0:DEC, 8:9]).then_inc(v_ss, 1)
                    act.wait_ge(v_ss, 9)
                    nc.scalar.activation(v_root[:, 0:8], v_sq[:, 0:8], ACT.Sqrt, bias=eps[:, 0:1],
                                         scale=1.0 / HALF).then_inc(v_rt, 1)
                    nc.scalar.activation(v_root[0:DEC, 8:9], v_sq[0:DEC, 8:9], ACT.Sqrt, bias=eps[0:DEC, 0:1],
                                         scale=1.0 / HALF).then_inc(v_rt, 1)

            out_squares(0, EVEN_OUT)
            end_phase(0)
            mlp(0, 1)

            first_pre(2)

            def odd_chunk(c, q, p):
                act.wait_ge(cp_ok, 4 * c + 4)
                act.wait_ge(cpad_in, 16 * c + 16)
                nc.scalar.copy(c_tail[:, 0, ds(c, 1), :], cp[q][:, SEQ:SEQ + CC - 1].unsqueeze(1)).then_inc(ctails, 1)
                nc.scalar.copy(c_tail[:, 1, ds(c, 1), :], cp[q][:, PB - (CC - 1):PB].unsqueeze(1)).then_inc(ctails, 1)
                for t in range(NT):
                    for j, (o0, n, tok, smp) in enumerate(tile_pieces(t)):
                        act.wait_ge(mix_mul, 24 + 4 * c + t + j + 1)
                        y = cy[q][:, (PS if smp else tok):(PS if smp else tok) + n]
                        nc.scalar.copy(h_hi[:, ds(c * TOK + tok, n)], y).then_inc(mix_high, 1)

            with act.Fori(0, KC // 2) as i:
                for q2 in range(2):
                    odd_chunk(2 * i + q2, q2, ODD_IN + 6 * i + 3 * q2 + 2)
            out_squares(2, ODD_OUT)
            end_phase(2)
            mlp(1, 3)

            for n in range(9):
                w = P if n < 8 else DEC
                dst = y_rows[:, n, 512:D] if n < 8 else y_rows_s[:, 512:D]
                act.wait_ge(y_pe, 2 * n + 2)
                nc.scalar.copy(dst, ps[0:w, 2 * (n % 3) + 1, :]).then_inc(y_b, 1)

        @block.vector
        def _(dve):
            steps = [0]

            def link(ins):
                ins.then_inc(soft_ok, 1)
                steps[0] += 1
                dve.wait_ge(soft_ok, steps[0])

            dve.wait_ge(soft_act, 2)
            e, z, z2, poly = soft[:, 1, :], soft[:, 2, :], soft[:, 3, :], soft[:, 4, :]
            link(nc.vector.tensor_scalar(soft[:, 0, :], e, 2.0, None, ALU.add))
            link(nc.vector.reciprocal(soft[:, 5, :], soft[:, 0, :]))
            link(nc.vector.tensor_tensor(z, e, soft[:, 5, :], ALU.mult))
            link(nc.vector.tensor_tensor(z2, z, z, ALU.mult))
            link(nc.vector.tensor_scalar(poly, z2, 1.0 / 15, 1.0 / 13, ALU.mult, ALU.add))
            for odd in (11, 9, 7, 5, 3, 1):
                link(nc.vector.tensor_tensor(poly, poly, z2, ALU.mult))
                link(nc.vector.tensor_scalar(poly, poly, 1.0 / odd, None, ALU.add))
            link(nc.vector.tensor_tensor(poly, poly, z, ALU.mult))
            link(nc.vector.tensor_scalar(soft[:, 6, :], b_vec[:, 3, :], -1.0, 0.0, ALU.mult, ALU.max))
            link(nc.vector.scalar_tensor_tensor(soft[:, 6, :], poly, 2.0, soft[:, 6, :], ALU.mult, ALU.add))
            link(nc.vector.tensor_scalar(soft[:, 7, :], soft[:, 6, :], 4.0, None, ALU.mult))
            assert steps[0] == SOFT_STEPS

            def factors(n, t):
                dve.wait_ge(rooted, n + 1)
                wait(dve, diag, n)
                nc.vector.reciprocal(rcol[0:JW, :], root[0:JW, :]).then_inc(inverted, 1)
                dve.wait_ge(inverted, n + 1)
                nc.vector.tensor_tensor(tmp[t][0:JW, :].rearrange("p (j c) -> p j c", j=NJ),
                                        ident[0:JW, 0:JW].unsqueeze(1).to_broadcast([JW, NJ, JW]),
                                        rcol[0:JW, :].unsqueeze(2).to_broadcast([JW, NJ, JW]),
                                        ALU.mult).then_inc(diag, 1)

            def scaled(dst, p, s, t, first=None):
                dve.wait_ge(pe_tile, 3 * p + t + 1)
                if first is not None:
                    dve.wait_ge(rs_ready, pre_n(first, t) + 1)
                return nc.vector.tensor_tensor(dst, bank(s, t), rstd[:, t * TT:(t + 1) * TT], ALU.mult)

            def add_squares(u, t, k):
                n = 21 * u + 7 * t + k
                dve.wait_ge(upd_act, 2 * (24 * u + 8 * t + k + 1))
                dst = sq_sum[:, t * TT:(t + 1) * TT]
                if k > 1:
                    dve.wait_ge(upd_acc, n - 1)
                a = pt(f, 0, t) if k == 1 else dst
                nc.vector.tensor_tensor(dst, a, pt(f, k, t), ALU.add).then_inc(upd_acc, 1)

            def add_out(b, p, s, m, t, copy, stat):
                dve.wait_ge(pe_tile, 3 * p + t + 1)
                if copy:
                    nc.vector.tensor_copy(pt(f, m, t), bank(s, t)).then_inc(evac, 1)
                else:
                    dve.wait_ge(evac, 3 * p - 45 + t + 1 - 3)
                    nc.vector.tensor_tensor(pt(f, m, t), bank(s, t), pt(f, m, t), ALU.add).then_inc(evac, 1)
                if stat:
                    n = 24 * b + 3 * m + t
                    dst = sq_sum[:, t * TT:(t + 1) * TT]
                    dve.wait_ge(f_sq, n + 1)
                    if isinstance(m, int) and m == 0:
                        nc.vector.tensor_copy(dst, tmp[t][:, :]).then_inc(f_acc, 1)
                    else:
                        dve.wait_ge(f_acc, n - 2)
                        nc.vector.tensor_tensor(dst, dst, tmp[t][:, :], ALU.add).then_inc(f_acc, 1)

            def out_chunks(b, base, copy, stat, last):
                if stat:
                    for m in range(2):
                        for t in range(NT):
                            add_out(b, base + m, m, m, t, copy, stat)
                    with dve.Fori(1, 3) as i:
                        for s in range(2):
                            for t in range(NT):
                                add_out(b, base + 2 * i + s, s, 2 * i + s, t, copy, stat)
                    for t in range(NT):
                        add_out(b, base + 6, 0, 6, t, copy, stat)
                else:
                    with dve.Fori(0, 4) as i:
                        for s in range(2):
                            for t in range(NT):
                                add_out(b, base + 2 * i + s, s, 2 * i + s, t, copy, stat)

            def end_phase(b, copy):
                p = LAST[b]
                add_out(b, p, 1, 7, 0, copy, True)
                add_out(b, p, 1, 7, 1, copy, True)
                factors(post_n(b, 0), 0)
                add_out(b, p, 1, 7, 2, copy, True)
                factors(post_n(b, 1), 1)
                factors(post_n(b, 2), 2)
                for t in range(NT):
                    dve.wait_ge(rs_ready, post_n(b, t) + 1)
                    for k in range(KC + 3):
                        if k < KC:
                            nc.vector.scalar_tensor_tensor(pt(f, k, t), pt(f, k, t), gains[:, POST_GAIN[b], k:k + 1],
                                                           rstd[:, t * TT:(t + 1) * TT], ALU.mult, ALU.mult
                                                           ).then_inc(upd_a, 1)
                        if k >= 4 and b < 3:
                            add_squares(b + 1, t, k - 3)

            def relu(p, s, n0, t, first=None):
                dve.wait_ge(pe_tile, 3 * p + t + 1)
                if first is not None:
                    dve.wait_ge(rs_ready, pre_n(first, t) + 1)
                wait(dve, h_ready, n0 + t - 2)
                nc.vector.scalar_tensor_tensor(tmp[t][:, :], bank(s, t), 0.0, rstd[:, t * TT:(t + 1) * TT],
                                               ALU.max, ALU.mult).then_inc(evac, 1)

            def h_low(n0, c, t):
                dve.wait_ge(h_high, n0 + t + 1)
                nc.vector.tensor_tensor(pt(h_lo, c, t), tmp[t][:, :], pt(h_hi, c, t).bitcast(F32),
                                        ALU.subtract).then_inc(h_ready, 1)

            def up_chunk(n0, p, s, c, first=None):
                for t in range(NT):
                    if first is not None:
                        factors(pre_n(first, t), t)
                    relu(p, s, n0, t, first)
                    h_low(n0, c, t)

            def mlp(l, u):
                for g in range(GROUPS):
                    base = MLP[l] + 16 * g
                    n0 = 96 * l + 24 * g
                    if g == 0:
                        up_chunk(n0, base, 0, 0, u)
                        up_chunk(n0 + 3, base + 1, 1, 1)
                        with dve.Fori(1, 4) as i:
                            for s in range(2):
                                up_chunk(n0 + 6 * i + 3 * s, base + 2 * i + s, s, 2 * i + s)
                    else:
                        with dve.Fori(0, 4) as i:
                            for s in range(2):
                                up_chunk(n0 + 6 * i + 3 * s, base + 2 * i + s, s, 2 * i + s)
                    out_chunks(2 * l + 1, base + 8, g == 0, g == GROUPS - 1, False)
                end_phase(2 * l + 1, False)

            for k in range(KC):
                dve.wait_ge(x0_t, k + 1)
                nc.vector.tensor_copy(x_sum[:, k * TOK:k * TOK + 512], ps[:, 2 * (k % 3), :]).then_inc(x0_a, 1)
            dve.wait_ge(x0_t, KC + 1)
            nc.vector.tensor_copy(x_sum[:, :].rearrange("p (k n) -> p k n", k=KC)[:, :, SEQ:TOK],
                                  ps[:, M0, 0:KC * DEC].rearrange("p (k n) -> p k n", k=KC)).then_inc(x0_a, 1)
            for t in range(NT):
                for k in range(1, KC):
                    add_squares(0, t, k)

            xc, q, ig, rc = lru

            def convolve(j):
                if j == 0:
                    dve.wait_ge(pad_in, 16 * HC)
                    dve.wait_ge(zeros, 2)
                else:
                    dve.wait_ge(lru_pool, 3 * j - 2)
                dve.wait_ge(evac, 3 * j + 3)
                nc.vector.tensor_scalar(xc[:, :], xb_pad[:, j, 0:LV], b_conv_w[:, 0, j:j + 1], b_vec[:, 0, j:j + 1],
                                        ALU.mult, ALU.add).then_inc(conv, 1)
                for r in range(1, CB):
                    dve.wait_ge(conv, 4 * j + r)
                    nc.vector.scalar_tensor_tensor(xc[:, :], xb_pad[:, j, r:r + LV], b_conv_w[:, r, j:j + 1], xc[:, :],
                                                   ALU.mult, ALU.add).then_inc(conv, 1)

            def decay(j):
                dve.wait_ge(lru_act, 2 * j + 1)
                if j > 0:
                    dve.wait_ge(scanned, 2 * j)
                nc.vector.tensor_scalar(rc[:, :], q[:, :], 1.0, None, ALU.add).then_inc(lru_dve, 1)
                dve.wait_ge(lru_dve, 3 * j + 1)
                nc.vector.reciprocal(rc[:, :], rc[:, :]).then_inc(lru_dve, 1)
                dve.wait_ge(lru_dve, 3 * j + 2)
                dve.wait_ge(lru_pool, 3 * j + 2)
                nc.vector.tensor_scalar(rc[:, :], rc[:, :], 2.0, -1.0, ALU.mult, ALU.add).then_inc(lru_dve, 1)

            def scan(j):
                dve.wait_ge(lru_dve, 3 * j + 3)
                dve.wait_ge(lru_pool, 3 * j + 3)
                nc.vector.tensor_tensor_scan(hr[:, j, 0:SEQ], rc[:, 0:SEQ], q[:, 0:SEQ], 0.0, ALU.mult,
                                             ALU.add).then_inc(scanned, 1)
                nc.vector.tensor_tensor_scan(hr[:, j, SEQ:TOK], rc[:, LS:LS + DEC], q[:, LS:LS + DEC],
                                             h_init[:, j:j + 1], ALU.mult, ALU.add).then_inc(scanned, 1)

            for p in range(16):
                if p >= 6:
                    dve.wait_ge(gelued, 3 * (p - 4))
                for t in range(NT):
                    first = 0 if p == 0 else None
                    if p == 0:
                        factors(pre_n(0, t), t)
                    if p < 4:
                        dve.wait_ge(pe_tile, 3 * p + t + 1)
                        if p == 0:
                            dve.wait_ge(rs_ready, t + 1)
                            dve.wait_ge(zeros, 2)
                        for j, (o0, n, tok, smp) in enumerate(tile_pieces(t)):
                            dst = LS + CB - 1 if smp else CB - 1 + tok
                            ins = nc.vector.tensor_tensor(xb_pad[:, p, dst:dst + n], ps[:, (p % 2) * NT + t, o0:o0 + n],
                                                          rstd[:, tok:tok + n], ALU.mult)
                        ins.then_inc(evac, 1)
                    else:
                        if p == 5:
                            dve.wait_ge(gelued, t + 1)
                        scaled(tmp[t][:, :], p, p % 2, t).then_inc(evac, 1)
                if p % 2 == 0 and p <= 8:
                    j = p // 2
                    if j > 0:
                        scan(j - 1)
                    if j < HC:
                        convolve(j)
                if p % 2 == 1 and p < 8:
                    decay(p // 2)
                if p == 9:
                    dve.wait_ge(v_rt, 2)
                    dve.wait_ge(s_in, 32)
                    nc.vector.reciprocal(v_rstd[:, 0:8], v_root[:, 0:8]).then_inc(v_inv, 1)
                    nc.vector.reciprocal(v_rstd[0:DEC, 8:9], v_root[0:DEC, 8:9]).then_inc(v_inv, 1)
                    dve.wait_ge(v_inv, 2)
                    for n in range(9):
                        rows = P if n < 8 else DEC
                        v = v_tok[:, n, :] if n < 8 else v_tok_s[:, :]
                        nc.vector.scalar_tensor_tensor(v, v, v_rstd[0:rows, n:n + 1], v_gain_bc[0:rows, :], ALU.mult,
                                                       ALU.mult).then_inc(v_ok, 1)
                if p == 10:
                    dve.wait_ge(b_in, 16)
                    for h in range(HC):
                        for part in range(3):
                            n = 3 * h + part
                            dve.wait_ge(sgu_pe, n + 1)
                            b = M0 + n % 2
                            if part < 2:
                                nc.vector.tensor_tensor(
                                    spatial[:, h, part * 512:(part + 1) * 512].rearrange("p (n i) -> p n i", n=4),
                                    ps[:, b, :].rearrange("p (n i) -> p n i", n=4),
                                    bias_bc[:, h:h + 1, :].to_broadcast([P, 4, P]), ALU.add).then_inc(sgu_ok, 1)
                            else:
                                nc.vector.tensor_tensor(spatial[:, h, SEQ:TOK], ps[:, b, 0:DEC], bias_bc[:, h, 0:DEC],
                                                        ALU.add).then_inc(sgu_ok, 1)

            out_chunks(0, EVEN_OUT, True, True, False)
            end_phase(0, True)
            mlp(0, 1)

            def odd_chunk(i, q, first):
                c = 2 * i + q
                for kind in range(3):
                    p = ODD_IN + 6 * i + 3 * q + kind
                    s = (3 * q + kind) % 2
                    for t in range(NT):
                        start = 2 if first and kind == 0 else None
                        if start is not None:
                            factors(pre_n(2, t), t)
                        if kind == 0:
                            if not first:
                                dve.wait_ge(cp_ok, 4 * c - 4)
                            scaled(cg[q][:, t * TT:(t + 1) * TT], p, s, t, start).then_inc(evac, 1)
                        elif kind == 1:
                            dve.wait_ge(mix_mul, 24 + 4 * c)
                            scaled(tmp[t][:, :], p, s, t).then_inc(evac, 1)
                        else:
                            dve.wait_ge(cp_ok, 4 * c + 4)
                            scaled(tmp[t][:, :], p, s, t).then_inc(evac, 1)
                    if kind == 1:
                        dve.wait_ge(cp_ok, 4 * c + 4)
                        dve.wait_ge(cpad_in, 16 * c + 16)
                        dve.wait_ge(mix_ready, 24 + 4 * c - (4 if not first else 0))
                        w = [c_conv_w[:, r, ds(c, 1)] for r in range(CC)]
                        nc.vector.tensor_scalar(cy[q][:, :], cp[q][:, 0:PV], w[0], None, ALU.mult).then_inc(cconv, 1)
                        for r in range(1, CC):
                            dve.wait_ge(cconv, 3 * c + r)
                            nc.vector.scalar_tensor_tensor(cy[q][:, :], cp[q][:, r:r + PV], w[r], cy[q][:, :], ALU.mult,
                                                           ALU.add).then_inc(cconv, 1)

            odd_chunk(0, 0, True)
            odd_chunk(0, 1, False)
            with dve.Fori(1, KC // 2) as i:
                for q2 in range(2):
                    odd_chunk(i, q2, False)
            out_chunks(2, ODD_OUT, True, True, False)
            end_phase(2, True)
            mlp(1, 3)

            for n in range(9):
                w = P if n < 8 else DEC
                dst = y_rows[:, n, 0:512] if n < 8 else y_rows_s[:, 0:512]
                dve.wait_ge(y_pe, 2 * n + 1)
                nc.vector.tensor_copy(dst, ps[0:w, 2 * (n % 3), :]).then_inc(y_a, 1)


N_VEC = 8 + 4 + 1 + CB + CC
SOFT_STEPS = 5 + 12 + 4

_INS = ['x_prompt', 'x_sample', 'cache_b_conv', 'state_b_h', 'cache_c_conv', 'norm_mix_pre', 'norm_mix_post',
        'norm_ffn_pre', 'norm_ffn_post', 'w_in_even', 'a_v_gain', 'a_w_s', 'a_b_s', 'b_conv_w', 'b_conv_b', 'b_wa',
        'b_ba', 'b_wx', 'b_bx', 'b_lambda', 'w_out_even', 'c_w_in', 'c_conv_w', 'c_w_out', 'mlp_up', 'mlp_down']
_OUTS = [("y_prompt", (1, SEQ, D)), ("y_sample", (1, DEC, D)), ("v", (1, 1, DEC, HALF)),
         ("bconv_p", (1, 1, CB - 1, HALF)), ("bh_p", (1, 1, HALF)), ("cconv_p", (1, 1, CC - 1, D)),
         ("bconv_s", (1, 1, CB - 1, HALF)), ("bh_s", (1, 1, HALF)), ("cconv_s", (1, 1, CC - 1, D))]


def kernel(**inputs):
    import numpy as _np
    import concourse.bacc as _bacc
    from concourse import mybir as _mybir
    from concourse.bass_utils import run_bass_kernel_spmd as _run

    nc = _bacc.Bacc("TRN2", target_bir_lowering=False, num_devices=1)
    arrays, ins, outs = {}, {}, {}
    for name in _INS:
        a = _np.ascontiguousarray(inputs[name])
        arrays[f"in_{name}_dram"] = a
        ins[name] = nc.dram_tensor(f"in_{name}_dram", a.shape, _mybir.dt.from_np(a.dtype), kind="ExternalInput").ap()
    for name, shape in _OUTS:
        outs[name] = nc.dram_tensor(f"out_{name}_dram", shape, _mybir.dt.float32, kind="ExternalOutput").ap()
    build(nc, ins, outs)
    r = _run(nc, [arrays], core_ids=[0])
    return tuple(r.results[0][f"out_{name}_dram"] for name, _ in _OUTS)
```

```python
from contextlib import ExitStack

import concourse.bass as bass
from concourse import mybir

P = 128
D = 1024
SEQ = 1024
DEC = 32
TOK = SEQ + DEC
NT = 3
TT = TOK // NT
KC = D // P
FF = 4096
GROUPS = FF // D
HALF = D // 2
HC = HALF // P
EPS = 1e-6
CB = 4
CC = 3
NJ = 4
JW = TT // NJ

EVEN_IN = 0
EVEN_OUT = EVEN_IN + 16
MLP = [EVEN_OUT + 8, 0]
ODD_IN = MLP[0] + 16 * GROUPS
ODD_OUT = ODD_IN + 24
MLP[1] = ODD_OUT + 8
PANELS = MLP[1] + 16 * GROUPS

PAIRED = {EVEN_IN, EVEN_OUT + 6, MLP[0], MLP[0] + 62, ODD_IN, ODD_OUT + 6, MLP[1], MLP[1] + 62}


def done(p, t):
    if isinstance(p, int) and p - p % 2 in PAIRED:
        return 3 * (p - p % 2) + 2 * t + p % 2 + 1
    return 3 * p + t + 1


V_GAIN, V_CONV_B, V_BIAS, V_LAMBDA, V_H0 = 0, 64, 80, 92, 96
V_CONV_C, V_ROWS = 100, 124
T_CONV_B, T_H, T_CONV_C, T_COLS = 0, 24, 32, 64

LB = (CB - 1) + SEQ + (CB - 1) + DEC
LV = LB - (CB - 1)
LT = LV // 3
LS = SEQ + CB - 1
PB = (CC - 1) + SEQ + (CC - 1) + DEC
PV = PB - (CC - 1)
PS = SEQ + CC - 1

F32 = mybir.dt.float32
F32R = mybir.dt.float32r
ALU = mybir.AluOpType
ACT = mybir.ActivationFunctionType
ds = bass.ds


def tile_pieces(t):
    lo, hi = t * TT, (t + 1) * TT
    if hi <= SEQ:
        return [(0, TT, lo, False)]
    return [(0, SEQ - lo, lo, False), (SEQ - lo, hi - SEQ, SEQ, True)]


def build(nc, A, O):
    with ExitStack() as ctx:
        at_byte = [nc.sbuf_base + (-nc.sbuf_base) % 32]

        def place(name, shape, dt, offset=None):
            size = 4
            for n in shape[1:]:
                size *= n
            here = at_byte[0] if offset is None else offset
            if offset is None:
                at_byte[0] += size + (-size) % 32
            return nc.alloc_sbuf_tensor_at(name, shape, dt, offset=here)

        def sem(name):
            return ctx.enter_context(nc.semaphore(name))

        CH = KC * TOK
        x_hi = place("x_hi", [P, CH], F32R)
        at_x_lo = at_byte[0]
        x_lo = place("x_lo", [P, CH], F32R)
        x_sum = place("x_sum", [P, CH], F32, at_x_lo)
        at_h_hi = at_byte[0]
        h_hi = place("h_hi", [P, CH], F32R)
        at_h_lo = at_byte[0]
        h_lo = place("h_lo", [P, CH], F32R)
        at_f = at_byte[0]
        f = place("f", [P, CH], F32)
        w_raw = [place(f"w_raw{s}", [P, D], F32) for s in range(2)]
        w_hi = [place(f"w_hi{s}", [P, D], F32R) for s in range(2)]
        w_lo = [place(f"w_lo{s}", [P, D], F32R) for s in range(2)]
        sq_sum = place("sq_sum", [P, TOK], F32)
        rstd = place("rstd", [P, TOK], F32)
        tmp = [place(f"tmp{t}", [P, TT], F32) for t in range(NT)]
        ident = place("ident", [P, P], F32)
        ones = place("ones", [P, P], F32)
        eps = place("eps", [P, 1], F32)
        root = place("root", [P, NJ], F32)
        rcol = place("rcol", [P, NJ], F32)
        vecs = place("vecs", [P, V_ROWS], F32)
        caches = place("caches", [P, CACHE_ROWS], F32)
        soft = place("soft", [P, 9, HC], F32)
        tail = place("tail", [P, T_COLS], F32)
        tail_b = tail[:, T_CONV_B:T_H].rearrange("p (i r c) -> p i r c", i=2, c=HC)
        tail_c = tail[:, T_CONV_C:T_COLS].rearrange("p (i r c) -> p i r c", i=2, c=KC)
        cache_b = caches[:, 0:(CB - 1) * HC].rearrange("p (r c) -> p r c", c=HC)
        cache_c = caches[:, (CB - 1) * HC:CACHE_ROWS].rearrange("p (r c) -> p r c", c=KC)
        v_sq = place("v_sq", [P, 9], F32)
        v_root = place("v_root", [P, 9], F32)
        v_rstd = place("v_rstd", [P, 9], F32)

        x_rows = place("x_rows", [P, SEQ // P, D], F32, at_h_hi)
        x_rows_s = place("x_rows_s", [DEC, D], F32, at_h_lo)
        vec_rows = place("vec_rows", [V_ROWS, P], F32, at_h_lo + D * 4)
        cache_rows = place("cache_rows", [CACHE_ROWS, P], F32, at_h_lo + (D + P) * 4)
        gate_w = place("gate_w", [P, 2, HC, P], F32, at_h_hi)
        xb_pad = place("xb_pad", [P, HC, LB], F32, at_h_hi + 3 * TOK * 4)
        lru_t = place("lru_t", [P, LV], F32, at_h_hi + TOK * 4)
        v_tok = place("v_tok", [P, SEQ // P, HALF], F32, at_h_lo)
        hr = place("hr", [P, HC, TOK], F32, at_h_lo + HC * TOK * 4)
        lru_step = LV * 4 + (-LV * 4) % 32
        lru = [place(f"lru{i}", [P, LV], F32, at_f + i * lru_step) for i in range(4)]
        spatial = place("spatial", [P, HC, TOK], F32, at_f)
        o = at_f + 4 * lru_step
        gelu = [place(f"gelu{i}", [P, TOK], F32, o + i * TOK * 4) for i in range(2)]
        ws_raw = place("ws_raw", [P, HC, P], F32, o + TOK * 4)
        o += 2 * TOK * 4
        bias_bc = place("bias_bc", [P, HC, P], F32, o)
        v_tok_s = place("v_tok_s", [DEC, HALF], F32, o + HALF * 4)
        ws_t = place("ws_t", [P, HC, P], F32, o + 2 * HALF * 4)
        v_gain_bc = place("v_gain_bc", [P, HALF], F32, o + 3 * HALF * 4)
        assert o + 4 * HALF * 4 <= at_f + CH * 4
        cg = [place(f"cg{i}", [P, TOK], F32, at_f + i * TOK * 4) for i in range(2)]
        c_step = PB * 4 + (-PB * 4) % 32
        cp = [place(f"cp{i}", [P, PB], F32, at_f + 2 * TOK * 4 + i * c_step) for i in range(2)]
        cy = [place(f"cy{i}", [P, PV], F32, at_f + 2 * TOK * 4 + (2 + i) * c_step) for i in range(2)]
        y_rows = place("y_rows", [P, SEQ // P, D], F32, at_h_hi)
        y_rows_s = place("y_rows_s", [DEC, D], F32, at_h_lo)
        tail_rows = place("tail_rows", [T_COLS, P], F32, at_h_lo + D * 4)

        def vec(i, rows=P):
            return vecs[0:rows, ds(i, 1)] if not isinstance(i, int) else vecs[0:rows, i:i + 1]

        ps = ctx.enter_context(nc.psum_tensor("ps", [P, 8, 512], F32))
        M0, M1 = 6, 7

        w_in = [sem(f"w_in{s}") for s in range(2)]
        w_gained = sem("w_gained")
        w_high = sem("w_high")
        w_ready = sem("w_ready")
        pe_tile = sem("pe_tile")
        evac = sem("evac")
        x_in = [sem(f"x_in{n}") for n in range(9)]
        c_in = sem("c_in")
        c_t = sem("c_t")
        c_ok = sem("c_ok")
        s_in = sem("s_in")
        b_in = sem("b_in")
        g_in = sem("g_in")
        pad_in = sem("pad_in")
        cpad_in = sem("cpad_in")
        consts = sem("consts")
        zeros = sem("zeros")
        czeros = sem("czeros")
        soft_ok = sem("soft_ok")
        soft_act = sem("soft_act")
        x0_t = sem("x0_t")
        x0_sq = sem("x0_sq")
        x0_a = sem("x0_a")
        x0_b = sem("x0_b")
        col = sem("col")
        rooted = sem("rooted")
        inverted = sem("inverted")
        diag = sem("diag")
        bc = sem("bc")
        rs_ready = sem("rs_ready")
        f_sq = sem("f_sq")
        f_acc = sem("f_acc")
        xs = sem("xs")
        upd_a = sem("upd_a")
        upd_x = sem("upd_x")
        upd_act = sem("upd_act")
        x_ready = sem("x_ready")
        acc_pool = sem("acc_pool")
        acc_dve = sem("acc_dve")
        h_sq = sem("h_sq")
        h_high = sem("h_high")
        h_ready = sem("h_ready")
        conv = sem("conv")
        gate_pe = sem("gate_pe")
        gate_act = sem("gate_act")
        lru_act = sem("lru_act")
        lru_dve = sem("lru_dve")
        lru_pool = sem("lru_pool")
        scanned = sem("scanned")
        tails = sem("tails")
        gelued = sem("gelued")
        ws_pe = sem("ws_pe")
        ws_ok = sem("ws_ok")
        ws_masked = sem("ws_masked")
        vt_pe = sem("vt_pe")
        vt_ok = sem("vt_ok")
        v_ss = sem("v_ss")
        v_rt = sem("v_rt")
        v_inv = sem("v_inv")
        v_ok = sem("v_ok")
        sgu_pe = sem("sgu_pe")
        sgu_ok = sem("sgu_ok")
        mix_mul = sem("mix_mul")
        mix_high = sem("mix_high")
        mix_ready = sem("mix_ready")
        cp_ok = sem("cp_ok")
        cconv = sem("cconv")
        ctails = sem("ctails")
        y_pe = sem("y_pe")
        y_a = sem("y_a")
        y_b = sem("y_b")
        t_pe = sem("t_pe")
        t_ok = sem("t_ok")
        out_dma = sem("out_dma")

        G_MIX_PRE, G_FFN_PRE, G_MIX_POST, G_FFN_POST = 0, 2, 4, 6

        def pt(buf, c, t):
            return buf[:, ds(c * TOK + t * TT, TT)]

        def bank(p2, t):
            return ps[:, p2 * NT + t, 0:TT]

        def wait(eng, s, n):
            if not isinstance(n, int) or n > 0:
                eng.wait_ge(s, n)

        def post_n(b, t):
            return 3 + 6 * b + t

        def pre_n(u, t):
            return 6 * u + t

        LAST = [EVEN_OUT + 7, MLP[0] + 63, ODD_OUT + 7, MLP[1] + 63]
        POST_GAIN = [G_MIX_POST, G_FFN_POST, G_MIX_POST + 1, G_FFN_POST + 1]

        EVEN_COLS = [8 + j for j in range(4)] + [4 + j for j in range(4)] + [12 + j for j in range(4)] + list(range(4))

        def gained_index(p):
            if p < EVEN_OUT:
                return p
            if p < ODD_IN:
                return 16 + 8 * ((p - MLP[0]) // 16) + (p - MLP[0]) % 16
            if p < ODD_OUT:
                return 48 + p - ODD_IN
            return 72 + 8 * ((p - MLP[1]) // 16) + (p - MLP[1]) % 16

        def slots(eng, base, first, n, split_next, work, next_gained):
            inner, after = next_gained

            def gain_of(c):
                return None if inner is None else inner + c

            with eng.Fori(first // 2, n // 2 - 1) as i:
                for s in range(2):
                    c = 2 * i + s
                    split_next(base + c + 1, 1 - s, base // 2 + i + s + 1, gain_of(c + 1))
                    work(base + c, s, c)
            for c in (n - 2, n - 1):
                s = c % 2
                split_next(base + c + 1, 1 - s, (base + c + 1) // 2 + 1, gain_of(c + 1) if s == 0 else after)
                work(base + c, s, c)

        block = ctx.enter_context(nc.Block())

        @block.sync
        def _(sp):
            def panel_at(p, s, src):
                wait(sp, w_ready, p - 1)
                sp.dma_start(w_raw[s][:, :].rearrange("p (k n) -> p k n", k=KC), src).then_inc(w_in[s], 16)

            def rows(w, r0, c):
                return w[r0:r0 + D, ds(c * P, P)].rearrange("(k p) n -> p k n", p=P)

            w_even = A["w_in_even"][0]
            xp = A["x_prompt"][0].rearrange("(n p) d -> p n d", p=P)
            for n in range(SEQ // P):
                sp.dma_start(x_rows[:, n, :], xp[:, n, :]).then_inc(x_in[n], 16)
                if n in (2, 5):
                    panel_at(n // 3, n // 3, rows(w_even, 0, EVEN_COLS[n // 3]))
            sp.dma_start(x_rows_s[:, :], A["x_sample"][0]).then_inc(x_in[8], 16)

            sp.wait_ge(zeros, 2)
            for g, name in ((0, "b_wa"), (1, "b_wx")):
                for half in range(2):
                    src = A[name][0].rearrange("(c two) i j -> two i c j", two=2)[half]
                    q = 64 * half
                    sp.dma_start(gate_w[q:q + 64, g, :, q:q + 64], src).then_inc(g_in, 16)
            panel_at(2, 0, rows(w_even, 0, EVEN_COLS[2]))
            sp.wait_ge(acc_pool, 7)
            sp.wait_ge(acc_dve, 2)
            sp.dma_start(ws_raw[:, :, :], A["a_w_s"][0].rearrange("h i j -> i h j")).then_inc(s_in, 16)
            sp.dma_start(v_gain_bc[:, :], A["a_v_gain"].to_broadcast([P, HALF])).then_inc(s_in, 16)
            sp.dma_start(bias_bc[:, :, :], A["a_b_s"][0:1].to_broadcast([P, HC, P])).then_inc(b_in, 16)
            for p in range(3, 16):
                panel_at(p, p % 2, rows(w_even, 0, EVEN_COLS[p]))
            sp.wait_ge(v_ok, 9)
            sp.dma_start(O["v"][0, 0], v_tok_s[:, :]).then_inc(out_dma, 16)

            def pairs(base, n, w, r0, c0=0):
                with sp.Fori(0, n // 2) as i:
                    for s in range(2):
                        panel_at(base + 2 * i + s, s, rows(w, r0, c0 + 2 * i + s))

            def mlp_loads(l):
                for g in range(GROUPS):
                    pairs(MLP[l] + 16 * g, 8, A["mlp_up"][l], 0, 8 * g)
                    pairs(MLP[l] + 16 * g + 8, 8, A["mlp_down"][l], g * D)

            pairs(EVEN_OUT, 8, A["w_out_even"][0], 0)
            mlp_loads(0)
            with sp.Fori(0, KC // 2) as i:
                for q in range(6):
                    part = (1, 2, 0)[q % 3]
                    panel_at(ODD_IN + 6 * i + q, q % 2, rows(A["c_w_in"][0], 0, part * KC + 2 * i + q // 3))
            pairs(ODD_OUT, 8, A["c_w_out"][0], 0)
            mlp_loads(1)

            sp.wait_ge(t_ok, 1)
            r = 0
            for name, n, chunks in (("bconv_p", CB - 1, HC), ("bconv_s", CB - 1, HC), ("bh_p", 1, HC), ("bh_s", 1, HC),
                                    ("cconv_p", CC - 1, KC), ("cconv_s", CC - 1, KC)):
                dst = O[name][0] if n == 1 else O[name][0, 0]
                sp.dma_start(dst.rearrange("r (c p) -> (r c) p", p=P), tail_rows[r:r + n * chunks, :]
                             ).then_inc(out_dma, 16)
                r += n * chunks
            yp = O["y_prompt"][0].rearrange("(n p) d -> p n d", p=P)
            for n in range(SEQ // P):
                sp.wait_ge(y_a, n + 1)
                sp.wait_ge(y_b, n + 1)
                sp.dma_start(yp[:, n, :], y_rows[:, n, :]).then_inc(out_dma, 16)
            sp.wait_ge(y_a, 9)
            sp.wait_ge(y_b, 9)
            sp.dma_start(O["y_sample"][0], y_rows_s[:, :]).then_inc(out_dma, 16)
            sp.wait_ge(out_dma, 16 * (1 + 6 + SEQ // P + 1))

        @block.gpsimd
        def _(pool):
            nc.gpsimd.memset(ones[:, :], 1.0).then_inc(consts, 1)
            nc.gpsimd.memset(ident[:, :], 0.0).then_inc(consts, 1)
            nc.gpsimd.memset(eps[:, :], EPS).then_inc(consts, 1)
            pool.wait_ge(consts, 3)
            nc.gpsimd.affine_select(out=ident[:, :], in_=ident[:, :], compare_op=ALU.not_equal, fill=1.0, base=0,
                                    pattern=[[-1, P]], channel_multiplier=1).then_inc(consts, 1)

            def gain(s, load, g):
                pool.wait_ge(w_in[s], 16 * load)
                raw = w_raw[s][:, :].rearrange("p (k n) -> p k n", k=KC)
                vector = vecs[:, V_GAIN + g * KC:V_GAIN + (g + 1) * KC]
                nc.gpsimd.tensor_tensor(raw, raw, vector.unsqueeze(2).to_broadcast([P, KC, P]),
                                        ALU.mult).then_inc(w_gained, 1)

            def gain_of(p, g):
                gain(p % 2, p // 2 + 1, g)

            def join_x(b, last):
                pool.wait_ge(pe_tile, done(last, 2))
                for k in range(KC):
                    c = slice(k * TOK, (k + 1) * TOK)
                    nc.gpsimd.tensor_tensor(x_sum[:, c], x_hi[:, c].bitcast(F32), x_lo[:, c].bitcast(F32),
                                            ALU.add).then_inc(xs, 1)

            def add_f(b, t):
                for k in range(KC):
                    pool.wait_ge(upd_a, 24 * b + 8 * t + k + 1)
                    pool.wait_ge(xs, 8 * b + k + 1)
                    nc.gpsimd.tensor_tensor(pt(x_sum, k, t), pt(x_sum, k, t), pt(f, k, t), ALU.add).then_inc(upd_x, 1)

            def sum_squares(u):
                dst = sq_sum[:, TT:2 * TT]
                for k in range(1, KC):
                    pool.wait_ge(upd_act, 2 * (24 * u + 8 + k + 1))
                    wait(pool, acc_pool, 7 * u + k - 1)
                    a = pt(f, 0, 1) if k == 1 else dst
                    nc.gpsimd.tensor_tensor(dst, a, pt(f, k, 1), ALU.add).then_inc(acc_pool, 1)

            def update(b, next_panel=None, g=None):
                for t in range(NT):
                    add_f(b, t)
                if b < 3:
                    gain_of(next_panel + 2, g)
                    sum_squares(b + 1)

            pool.wait_ge(x0_a, 3)
            pool.wait_ge(x0_b, 3)
            for k in range(KC):
                nc.gpsimd.tensor_tensor(pt(f, k, 0), pt(x_sum, k, 0), pt(x_sum, k, 0), ALU.mult).then_inc(x0_sq, 1)
            pool.wait_ge(c_ok, 1)
            gain_of(0, G_MIX_PRE)
            gain_of(1, G_MIX_PRE)
            pool.wait_ge(x0_t, 10)
            nc.gpsimd.memset(gate_w[:, :, :, :], 0.0).then_inc(zeros, 1)
            nc.gpsimd.memset(xb_pad[:, :, 0:CB - 1], 0.0).then_inc(zeros, 1)
            gain_of(2, G_MIX_PRE)
            sum_squares(0)
            gain_of(3, G_MIX_PRE)

            xc, q, ig, rc = lru
            for p in range(2, 16):
                if p + 2 < 16:
                    gain_of(p + 2, G_MIX_PRE)
                if p == 2:
                    pool.wait_ge(ws_ok, 1)
                    pool.wait_ge(w_gained, 5)
                    nc.gpsimd.memset(ws_t[64:P, :, 0:64], 0.0).then_inc(ws_masked, 1)
                    pool.wait_ge(ws_masked, 1)
                if p in (3, 5, 7, 9):
                    j = (p - 3) // 2
                    pool.wait_ge(gate_act, 6 * j + 6)
                    nc.gpsimd.tensor_tensor(ig[:, :], ig[:, :], xc[:, :], ALU.mult).then_inc(lru_pool, 1)
                if p in (4, 6, 8, 10):
                    j = p // 2 - 2
                    pool.wait_ge(lru_act, 3 * j + 3)
                    pool.wait_ge(lru_dve, 4 * j + 3)
                    nc.gpsimd.tensor_tensor(q[:, :], q[:, :], lru_t[:, :], ALU.mult).then_inc(lru_pool, 1)
                    pool.wait_ge(lru_pool, 3 * j + 2)
                    nc.gpsimd.tensor_tensor(q[:, :], q[:, :], ig[:, :], ALU.mult).then_inc(lru_pool, 1)
                if p >= 8:
                    c = p - 8
                    buf, m = (hr, c) if c < 4 else (spatial, c - 4)
                    ch = 4 + c if c < 4 else c - 4
                    for t in range(NT):
                        n = 3 * c + t
                        tile = buf[:, m, t * TT:(t + 1) * TT]
                        pool.wait_ge(gelued, 12 + n + 1)
                        if c < 4 and t == 0:
                            pool.wait_ge(scanned, 2 * c + 2)
                            pool.wait_ge(tails, 2 * HC + 2 * c + 2)
                        if c >= 4 and t == 0:
                            pool.wait_ge(sgu_ok, 3 * (c - 4) + 3)
                        nc.gpsimd.tensor_tensor(tile, tile, gelu[p % 2][:, t * TT:(t + 1) * TT],
                                                ALU.mult).then_inc(mix_mul, 1)
                        pool.wait_ge(mix_mul, n + 1)
                        pool.wait_ge(mix_high, n + 1)
                        nc.gpsimd.tensor_tensor(pt(h_lo, ch, t), tile, pt(h_hi, ch, t).bitcast(F32),
                                                ALU.subtract).then_inc(mix_ready, 1)

            def mlp_gains(l):
                g, base = G_FFN_PRE + l, MLP[l]
                gain_of(base + 3, g)
                with pool.Fori(2, 4) as i:
                    for s in range(2):
                        gain(s, base // 2 + 1 + i, g)
                for group in range(1, GROUPS):
                    with pool.Fori(0, 4) as i:
                        for s in range(2):
                            gain(s, base // 2 + 8 * group + 1 + i, g)

            def end_phase(b, last_read, next_panel=None, g=None):
                join_x(b, last_read)
                if b < 3:
                    gain_of(next_panel, g)
                    gain_of(next_panel + 1, g)
                update(b, next_panel, g)

            end_phase(0, EVEN_OUT - 1, MLP[0], G_FFN_PRE)
            mlp_gains(0)
            end_phase(1, MLP[0] + 55, ODD_IN, G_MIX_PRE + 1)
            pool.wait_ge(acc_pool, 7 * 3)
            pool.wait_ge(acc_dve, 2 * 3)
            for i in range(2):
                nc.gpsimd.memset(cp[i][:, 0:CC - 1], 0.0).then_inc(czeros, 1)

            def odd_panel(p, s, c, q, kind, load):
                if load is not None:
                    gain(1 - s, load, G_MIX_PRE + 1)
                if kind == 1:
                    for t in range(NT):
                        pool.wait_ge(evac, done(p, t))
                        for (o0, n, tok, smp) in tile_pieces(t):
                            dst = (PS + CC - 1) if smp else (CC - 1 + tok)
                            nc.gpsimd.tensor_tensor(cp[q][:, dst:dst + n], tmp[t][:, o0:o0 + n], cg[q][:, tok:tok + n],
                                                    ALU.mult).then_inc(cp_ok, 1)
                if kind == 2:
                    pool.wait_ge(cconv, 3 * c + 3)
                    for t in range(NT):
                        pool.wait_ge(evac, done(p, t))
                        for j, (o0, n, tok, smp) in enumerate(tile_pieces(t)):
                            y = cy[q][:, (PS if smp else tok):(PS if smp else tok) + n]
                            m = 24 + 4 * c + t + j
                            nc.gpsimd.tensor_tensor(y, tmp[t][:, o0:o0 + n], y, ALU.mult).then_inc(mix_mul, 1)
                            pool.wait_ge(mix_mul, m + 1)
                            pool.wait_ge(mix_high, m + 1)
                            lo, hi = h_lo[:, ds(c * TOK + tok, n)], h_hi[:, ds(c * TOK + tok, n)]
                            nc.gpsimd.tensor_tensor(lo, y, hi.bitcast(F32), ALU.subtract).then_inc(mix_ready, 1)

            def odd_pair_of_chunks(i):
                for q in range(6):
                    load = ODD_IN // 2 + 3 * i + (q + 1) // 2 + 1
                    if isinstance(i, int) and ((i == 0 and q < 2) or (i == KC // 2 - 1 and q == 5)):
                        load = None
                    odd_panel(ODD_IN + 6 * i + q, q % 2, 2 * i + q // 3, q // 3, q % 3, load)

            odd_pair_of_chunks(0)
            with pool.Fori(1, KC // 2 - 1) as i:
                odd_pair_of_chunks(i)
            odd_pair_of_chunks(KC // 2 - 1)
            end_phase(2, ODD_OUT - 1, MLP[1], G_FFN_PRE + 1)
            mlp_gains(1)
            end_phase(3, MLP[1] + 55)

        @block.tensor
        def _(pe):
            X, H = (x_hi, x_lo), (h_hi, h_lo)
            IN_ORDER = tuple(range(KC))

            def tile(p, s, src, t, before=None, mid=None, order=IN_ORDER):
                wait(pe, evac, 3 * p - 5 + (2 * t if s == 0 else t))
                for i, k in enumerate(order):
                    if before:
                        before(t, k)
                    hi, lo = pt(src[0], k, t), pt(src[1], k, t)
                    wh, wl = w_hi[s][:, k * P:(k + 1) * P], w_lo[s][:, k * P:(k + 1) * P]
                    dst = bank(s, t)
                    nc.tensor.matmul(dst, wh, hi, start=(i == 0), stop=False)
                    nc.tensor.matmul(dst, wh, lo, start=False, stop=False)
                    last = nc.tensor.matmul(dst, wl, hi, start=False, stop=(i == KC - 1))
                    if i == KC - 1:
                        last.then_inc(pe_tile, 1)
                    if mid:
                        mid(t, i)

            def panel(p, s, src, before=None, mid=None, order=IN_ORDER):
                pe.wait_ge(w_ready, p + 1)
                for t in range(NT):
                    tile(p, s, src, t, before, mid, order)

            def pairs(base, first, n, src, before=None):
                with pe.Fori(first, n) as i:
                    for s in range(2):
                        panel(base + 2 * i + s, s, src, before=before if s == 0 else None)

            def col_sums(n, t):
                wait(pe, rooted, n)
                for j in range(NJ):
                    c0 = t * TT + j * JW
                    last = nc.tensor.matmul(ps[0:JW, M0, j:j + 1], sq_sum[:, c0:c0 + JW], ones[:, 0:1],
                                            start=True, stop=True)
                last.then_inc(col, 1)

            def spread(n, t):
                pe.wait_ge(diag, n + 1)
                wait(pe, rs_ready, n)
                nc.tensor.matmul(ps[:, M1, 0:TT], ones[0:JW, :], tmp[t][0:JW, :], start=True, stop=True).then_inc(bc, 1)

            def post_sums(b, t):
                pe.wait_ge(f_acc, 24 * b + 18 + 2 * t + 2)
                col_sums(post_n(b, t), t)

            def pre_sums(u, t):
                if t == 1:
                    pe.wait_ge(acc_pool, 7 * u + 7)
                else:
                    pe.wait_ge(acc_dve, 2 * u + 1 + t // 2)
                col_sums(pre_n(u, t), t)

            def last_pair(b):
                p = LAST[b] - 1

                def mid(t, i):
                    if t > 0 and i == 3:
                        post_sums(b, t - 1)
                    if t > 0 and i == 6:
                        spread(post_n(b, t - 1), t - 1)

                pe.wait_ge(w_ready, p + 1)
                for t in range(NT):
                    tile(p, 0, H, t, mid=mid)
                    if t == 0:
                        pe.wait_ge(w_ready, p + 2)
                    tile(p + 1, 1, H, t)

            def first_pair(base, u, after_pair=None):
                def before(t, k):
                    pe.wait_ge(x_ready, 24 * u + 8 * t + k + 1)

                def mid(t, i):
                    if t == 0 and u > 0 and i == 3:
                        post_sums(u - 1, 2)
                    if t == 0 and u > 0 and i == 6:
                        spread(post_n(u - 1, 2), 2)

                def mid2(t, i):
                    if t == 2 and i == 2:
                        pre_sums(u, 0)
                    if t == 2 and i == 6:
                        spread(pre_n(u, 0), 0)

                def mid3(t, i):
                    if t == 0 and i == 3:
                        pre_sums(u, 1)
                    if t == 0 and i == 7:
                        spread(pre_n(u, 1), 1)
                    if t == 1 and i == 2:
                        pre_sums(u, 2)
                    if t == 1 and i == 6:
                        spread(pre_n(u, 2), 2)

                pe.wait_ge(w_ready, base + 1)
                for t in range(NT):
                    tile(base, 0, X, t, before=before, mid=mid)
                    if t == 0:
                        pe.wait_ge(w_ready, base + 2)
                    tile(base + 1, 1, X, t, mid=mid2)
                panel(base + 2, 0, X, mid=mid3)

            def mlp(l, u):
                for g in range(GROUPS):
                    base = MLP[l] + 16 * g
                    if g == 0:
                        first_pair(base, u)
                        panel(base + 3, 1, X)
                        pairs(base, 2, 4, X)
                    else:
                        pairs(base, 0, 4, X)
                    done_before = 96 * l + 24 * g

                    def before(t, k, n=done_before):
                        if k == 0 and t == 0:
                            pe.wait_ge(h_ready, n + 21)
                        if k == KC - 1:
                            pe.wait_ge(h_ready, n + 21 + t + 1)
                    pairs(base + 8, 0, 4 if g < GROUPS - 1 else 3, H, before)
                last_pair(2 * l + 1)

            pe.wait_ge(consts, 4)
            for n in range(SEQ // P):
                pe.wait_ge(x_in[n], 16)
                a = 2 * (n % 3)
                wait(pe, x0_a, n - 2)
                wait(pe, x0_b, n - 2)
                for k in range(KC):
                    last = nc.tensor.transpose(ps[:, a + k // 4, (k % 4) * P:(k % 4 + 1) * P],
                                               x_rows[:, n, k * P:(k + 1) * P], ident[:, :])
                last.then_inc(x0_t, 1)
                if n == 5:
                    pe.wait_ge(c_in, 16 * len(VEC_SRC))
                    nc.tensor.transpose(ps[:, M1, 0:V_ROWS], vec_rows[:, :], ident[0:V_ROWS, 0:V_ROWS]).then_inc(c_t, 1)
            pe.wait_ge(x_in[8], 16)
            for k in range(KC):
                last = nc.tensor.transpose(ps[:, M0, k * DEC:(k + 1) * DEC], x_rows_s[:, k * P:(k + 1) * P],
                                           ident[0:DEC, 0:DEC])
            last.then_inc(x0_t, 1)
            pe.wait_ge(c_ok, 1)
            nc.tensor.transpose(ps[:, M1, 0:CACHE_ROWS], cache_rows[:, :], ident[0:CACHE_ROWS, 0:CACHE_ROWS]
                                ).then_inc(c_t, 1)
            pe.wait_ge(c_ok, 2)
            pe.wait_ge(x0_a, 9)
            pe.wait_ge(x0_b, 8)
            nc.tensor.transpose(ps[:, M1, 0:P], ident[:, :], ident[:, :]).then_inc(x0_t, 1)

            def even_after(p):
                if p == 2:
                    pe.wait_ge(s_in, 32)
                    pe.wait_ge(rs_ready, 3)
                    for h in range(HC):
                        last = nc.tensor.transpose(ps[:, M1, h * P:(h + 1) * P], ws_raw[:, h, :], ident[:, :])
                    last.then_inc(ws_pe, 1)
                if p == 11:
                    pe.wait_ge(v_ok, 9)
                    pe.wait_ge(ws_masked, 1)
                    for h in range(HC):
                        for part in range(3):
                            n = 3 * h + part
                            wait(pe, sgu_ok, n - 1)
                            b = M0 + n % 2
                            if part < 2:
                                for q in range(4):
                                    m = 4 * part + q
                                    last = nc.tensor.matmul(ps[:, b, q * P:(q + 1) * P], v_tok[:, m, h * P:(h + 1) * P],
                                                            ws_t[:, h, :], start=True, stop=True)
                            else:
                                last = nc.tensor.matmul(ps[:, b, 0:DEC], v_tok_s[:, h * P:(h + 1) * P],
                                                        ws_t[0:DEC, h, 0:DEC], start=True, stop=True)
                            last.then_inc(sgu_pe, 1)

            def gate(j, n):
                g, t = 1 - n // 3, n % 3
                n += 6 * j
                if n == 6 * j:
                    pe.wait_ge(g_in, 64)
                    pe.wait_ge(ws_ok, 1)
                    pe.wait_ge(conv, 4 * j + 4)
                    wait(pe, vt_ok, 3 * (2 * j - 2))
                wait(pe, gate_act, n - 1)
                nc.tensor.matmul(ps[:, M0 + n % 2, 0:LT], gate_w[:, g, j, :], lru[0][:, t * LT:(t + 1) * LT],
                                 start=True, stop=True).then_inc(gate_pe, 1)

            def values_to_rows(c, half):
                g = gelu[c % 2]
                if half == 0:
                    pe.wait_ge(gate_act, 6 * ((c + 4) // 2))
                    wait(pe, vt_ok, 3 * c)
                    pe.wait_ge(gelued, 3 * c + 3)
                if half < 2:
                    for n in range(4):
                        m = 4 * half + n
                        last = nc.tensor.transpose(ps[:, M0 + half, n * P:(n + 1) * P], g[:, m * P:(m + 1) * P],
                                                   ident[:, :])
                else:
                    pe.wait_ge(vt_ok, 3 * c + 1)
                    last = nc.tensor.transpose(ps[0:DEC, M0, 0:P], g[:, SEQ:TOK], ident[:, :])
                last.then_inc(vt_pe, 1)

            def even_mid(p):
                gates = [(0, 5), (0, 7), (1, 1), (1, 3), (1, 5), (1, 7)]
                values = [(2, 2), (2, 4), (2, 7)]

                def mid(t, i):
                    if p in (3, 5, 7, 9) and (t, i) in gates:
                        gate((p - 3) // 2, gates.index((t, i)))
                    if 5 <= p < 9 and (t, i) in values:
                        values_to_rows(p - 5, values.index((t, i)))
                return mid

            first_pair(EVEN_IN, 0)
            even_after(2)
            for p in range(3, 16):
                panel(p, p % 2, X, mid=even_mid(p))
                even_after(p)

            EVEN_ORDER = (4, 5, 6, 7, 0, 1, 2, 3)

            def before_even(t, k):
                if k == EVEN_ORDER[0] and t == 0:
                    pe.wait_ge(mix_ready, 21)
                if k == HC - 1:
                    pe.wait_ge(mix_ready, 21 + t + 1)

            panel(EVEN_OUT, 0, H, before=before_even, order=EVEN_ORDER)
            panel(EVEN_OUT + 1, 1, H)
            pairs(EVEN_OUT, 1, 3, H)
            last_pair(0)
            mlp(0, 1)

            first_pair(ODD_IN, 2)
            panel(ODD_IN + 3, 1, X)
            pairs(ODD_IN, 2, 12, X)

            def before_odd(t, k):
                if k == 0 and t == 0:
                    pe.wait_ge(mix_ready, 24 + 28)
                if k == KC - 1:
                    pe.wait_ge(mix_ready, 24 + 28 + (1, 2, 4)[t])

            panel(ODD_OUT, 0, H, before=before_odd)
            panel(ODD_OUT + 1, 1, H)
            pairs(ODD_OUT, 1, 3, H)
            last_pair(2)
            mlp(1, 3)

            post_sums(3, 2)
            spread(post_n(3, 2), 2)
            pe.wait_ge(rooted, post_n(3, 2) + 1)
            nc.tensor.transpose(ps[0:T_COLS, M0, 0:P], tail[:, :], ident[:, :]).then_inc(t_pe, 1)
            pe.wait_ge(evac, 3 * PANELS)
            for n in range(9):
                w = P if n < 8 else DEC
                t_end = (n * P + w - 1) // TT
                pe.wait_ge(upd_x, 24 * 3 + 8 * t_end + 8)
                wait(pe, y_a, n - 2)
                wait(pe, y_b, n - 2)
                for k in range(KC):
                    last = nc.tensor.transpose(ps[0:w, 2 * (n % 3) + k // 4, (k % 4) * P:(k % 4 + 1) * P],
                                               x_sum[:, k * TOK + n * P:k * TOK + n * P + w], ident[:, :])
                    if k % 4 == 3:
                        last.then_inc(y_pe, 1)

        @block.scalar
        def _(act):
            r = 0
            for name, n in VEC_SRC:
                src = A[name]
                if n > V_ROWS:
                    continue
                if name in ("cache_b_conv", "cache_c_conv"):
                    r0 = 0 if name == "cache_b_conv" else (CB - 1) * HC
                    act.dma_start(cache_rows[r0:r0 + n, :], src[0, 0].rearrange("r (c p) -> (r c) p", p=P)
                                  ).then_inc(c_in, 16)
                    continue
                flat = src[0] if name in ("state_b_h", "b_conv_w", "c_conv_w") else src
                act.dma_start(vec_rows[r:r + n, :], flat.rearrange("r (c p) -> (r c) p", p=P)).then_inc(c_in, 16)
                r += n

            def high(p, s, load, gained):
                if gained is None:
                    act.wait_ge(w_in[s], 16 * load)
                else:
                    act.wait_ge(w_gained, gained + 1)
                wait(act, pe_tile, done(p - 2, 2))
                nc.scalar.copy(w_hi[s][:, :], w_raw[s][:, :]).then_inc(w_high, 1)

            def high_of(p, has_gain):
                high(p, p % 2, p // 2 + 1, gained_index(p) if has_gain else None)

            def rs_root(n):
                act.wait_ge(col, n + 1)
                wait(act, inverted, n)
                nc.scalar.activation(root[0:JW, :], ps[0:JW, M0, 0:NJ], ACT.Sqrt, bias=eps[0:JW, 0:1],
                                     scale=1.0 / D).then_inc(rooted, 1)

            def rs_copy(n, t):
                act.wait_ge(bc, n + 1)
                nc.scalar.copy(rstd[:, t * TT:(t + 1) * TT], ps[:, M1, 0:TT]).then_inc(rs_ready, 1)

            def split_x(u, t, k0=0, k1=KC):
                for k in range(k0, k1):
                    if u > 0:
                        act.wait_ge(upd_x, 24 * (u - 1) + 8 * t + k + 1)
                    nc.scalar.copy(pt(x_hi, k, t), pt(x_sum, k, t)).then_inc(upd_act, 1)
                    nc.scalar.activation(pt(f, k, t), pt(x_sum, k, t), ACT.Square).then_inc(upd_act, 1)

            def square_out(n, p, m, t):
                act.wait_ge(evac, done(p, t))
                wait(act, f_acc, n - 1 if isinstance(p, int) and p - p % 2 in PAIRED else n - 2)
                nc.scalar.activation(tmp[t][:, :], pt(f, m, t), ACT.Square).then_inc(f_sq, 1)

            def out_squares(b, base):
                def work(p, s, c):
                    for t in range(NT):
                        square_out(24 * b + 3 * c + t, p, c, t)

                high_of(base + 1, False)
                work(base, 0, 0)
                high_of(base + 2, False)
                work(base + 1, 1, 1)
                slots(act, base, 2, 6, high, work, (None, None))

            def end_phase(b, next_panel=None):
                p = LAST[b] - 1
                n0 = 24 * b + 18

                def square_pair(t, s):
                    square_out(n0 + 2 * t + s, p + s, 6 + s, t)

                high_of(p + 1, False)
                square_pair(0, 0)
                square_pair(0, 1)
                rs_root(post_n(b, 0))
                rs_copy(post_n(b, 0), 0)
                square_pair(1, 0)
                if b < 3:
                    split_x(b + 1, 0, 0, 1)
                square_pair(1, 1)
                if b < 3:
                    split_x(b + 1, 0, 1, 3)
                rs_root(post_n(b, 1))
                if b < 3:
                    split_x(b + 1, 0, 3, 8)
                rs_copy(post_n(b, 1), 1)
                if b < 3:
                    high_of(next_panel, True)
                square_pair(2, 0)
                square_pair(2, 1)
                if b < 3:
                    high_of(next_panel + 1, True)
                    split_x(b + 1, 1, 0, 2)
                rs_root(post_n(b, 2))
                if b < 3:
                    split_x(b + 1, 1, 2, 4)
                rs_copy(post_n(b, 2), 2)
                if b < 3:
                    split_x(b + 1, 1, 4, 8)
                    split_x(b + 1, 2)

            def relu_split(n, p, c, t):
                act.wait_ge(evac, done(p, t))
                nc.scalar.activation(tmp[t][:, :], tmp[t][:, :], ACT.Square).then_inc(h_sq, 1)
                act.wait_ge(h_sq, n + 1)
                nc.scalar.copy(pt(h_hi, c, t), tmp[t][:, :]).then_inc(h_high, 1)

            def mlp(l, u, next_panel=None):
                for g in range(GROUPS):
                    base = MLP[l] + 16 * g
                    n0 = 96 * l + 24 * g

                    def work(p, s, c, n0=n0):
                        for t in range(NT):
                            relu_split(n0 + 3 * c + t, p, c, t)

                    if g == 0:
                        high_of(base + 2, True)
                        for t in range(NT):
                            rs_root(pre_n(u, t))
                            rs_copy(pre_n(u, t), t)
                            for s in range(2):
                                relu_split(n0 + 2 * t + s, base + s, s, t)
                    up = gained_index(base)
                    slots(act, base, 2 if g == 0 else 0, 8, high, work, (up, None))
                    d = base + 8
                    if g < GROUPS - 1:
                        slots(act, d, 0, 8, high, lambda p, s, c: None, (None, up + 8))
                out_squares(2 * l + 1, MLP[l] + 56)
                end_phase(2 * l + 1, next_panel)

            act.wait_ge(consts, 4)
            xk = x_sum[:, :].rearrange("p (k n) -> p k n", k=KC)
            for n in range(SEQ // P):
                act.wait_ge(x0_t, n + 1)
                nc.scalar.copy(xk[:, 4:8, n * P:(n + 1) * P],
                               ps[:, 2 * (n % 3) + 1, :].rearrange("p (k n) -> p k n", k=4)).then_inc(x0_b, 1)
                if n == 2:
                    act.wait_ge(x0_a, 3)
                    act.wait_ge(x0_b, 3)
                    for k in range(KC):
                        nc.scalar.copy(pt(x_hi, k, 0), pt(x_sum, k, 0)).then_inc(upd_act, 2)
                if n == 5:
                    act.wait_ge(c_t, 1)
                    nc.scalar.copy(vecs[:, :], ps[:, M1, 0:V_ROWS]).then_inc(c_ok, 1)
                    act.wait_ge(x0_a, 6)
                    act.wait_ge(x0_b, 6)
                    split_x(0, 1, 0, 4)
            act.wait_ge(c_t, 2)
            nc.scalar.copy(caches[:, :], ps[:, M1, 0:CACHE_ROWS]).then_inc(c_ok, 1)
            high_of(0, True)
            split_x(0, 1, 4, 8)
            high_of(1, True)
            act.wait_ge(x0_a, 9)
            act.wait_ge(x0_b, 8)
            split_x(0, 2)
            act.wait_ge(c_ok, 1)
            nc.scalar.activation(soft[:, 0, :], vecs[:, V_LAMBDA:V_LAMBDA + HC], ACT.Abs).then_inc(soft_act, 1)
            act.wait_ge(soft_act, 1)
            nc.scalar.activation(soft[:, 1, :], soft[:, 0, :], ACT.Exp, scale=-1.0).then_inc(soft_act, 1)

            def conv_rows(j):
                act.wait_ge(evac, done(j, 2))
                act.wait_ge(pad_in, 1)
                nc.scalar.copy(tail_b[:, 0, :, j], xb_pad[:, j, SEQ:SEQ + CB - 1]).then_inc(tails, 1)
                nc.scalar.copy(tail_b[:, 1, :, j], xb_pad[:, j, LB - (CB - 1):LB]).then_inc(tails, 1)

            xc, q, ig, rc = lru
            act.wait_ge(zeros, 2)
            act.wait_ge(c_ok, 2)
            nc.scalar.copy(xb_pad[:, :, LS:LS + CB - 1], cache_b.rearrange("p r c -> p c r")).then_inc(pad_in, 1)
            high_of(2, True)
            for t in range(NT):
                rs_root(pre_n(0, t))
                rs_copy(pre_n(0, t), t)
            for p in range(2, 16):
                high_of(p + 1, p + 1 < 16)
                if p == 10:
                    act.wait_ge(vt_ok, 12)
                    act.wait_ge(rs_ready, 3)
                    for n in range(8):
                        nc.scalar.activation(sq_sum[:, 0:HALF], v_tok[:, n, :], ACT.Square,
                                             accum_out=v_sq[:, n:n + 1]).then_inc(v_ss, 1)
                        act.wait_ge(v_ss, n + 1)
                    nc.scalar.activation(sq_sum[0:DEC, 0:HALF], v_tok_s[:, :], ACT.Square,
                                         accum_out=v_sq[0:DEC, 8:9]).then_inc(v_ss, 1)
                    act.wait_ge(v_ss, 9)
                    nc.scalar.activation(v_root[:, 0:8], v_sq[:, 0:8], ACT.Sqrt, bias=eps[:, 0:1],
                                         scale=1.0 / HALF).then_inc(v_rt, 1)
                    nc.scalar.activation(v_root[0:DEC, 8:9], v_sq[0:DEC, 8:9], ACT.Sqrt, bias=eps[0:DEC, 0:1],
                                         scale=1.0 / HALF).then_inc(v_rt, 1)
                if p == 2:
                    conv_rows(0)
                    conv_rows(1)
                    act.wait_ge(ws_pe, 1)
                    nc.scalar.copy(ws_t[:, :, :].rearrange("p h j -> p (h j)"), ps[:, M1, :]).then_inc(ws_ok, 1)
                if p in (2, 3):
                    conv_rows(p)
                if p in (3, 5, 7, 9):
                    j = (p - 3) // 2
                    act.wait_ge(gate_act, 6 * j + 6)
                    if j == 0:
                        act.wait_ge(soft_ok, SOFT_STEPS)
                    nc.scalar.activation(rc[:, :], q[:, :], ACT.Exp, scale=soft[:, 8, j:j + 1]).then_inc(lru_act, 1)
                    act.wait_ge(lru_act, 3 * j + 1)
                    nc.scalar.activation(q[:, :], q[:, :], ACT.Tanh, scale=soft[:, 7, j:j + 1]).then_inc(lru_act, 1)
                if 5 <= p < 9:
                    c = p - 5
                    for half in range(2):
                        act.wait_ge(vt_pe, 3 * c + half + 1)
                        nc.scalar.copy(v_tok[:, 4 * half:4 * half + 4, c * P:(c + 1) * P],
                                       ps[:, M0 + half, :].rearrange("p (n j) -> p n j", n=4)).then_inc(vt_ok, 1)
                if p in (3, 5, 7, 9):
                    j = (p - 3) // 2
                    act.wait_ge(lru_act, 3 * j + 2)
                    act.wait_ge(lru_dve, 4 * j + 2)
                    nc.scalar.activation(q[:, :], q[:, :], ACT.Sqrt, scale=4.0).then_inc(lru_act, 1)
                if 5 <= p < 9:
                    c = p - 5
                    act.wait_ge(vt_pe, 3 * c + 3)
                    nc.scalar.copy(v_tok_s[:, c * P:(c + 1) * P], ps[0:DEC, M0, 0:P]).then_inc(vt_ok, 1)
                if p in (5, 7, 9, 11):
                    j = (p - 5) // 2
                    act.wait_ge(scanned, 2 * j + 2)
                    nc.scalar.copy(tail[:, T_H + j:T_H + j + 1], hr[:, j, SEQ - 1:SEQ]).then_inc(tails, 1)
                    nc.scalar.copy(tail[:, T_H + HC + j:T_H + HC + j + 1], hr[:, j, TOK - 1:TOK]).then_inc(tails, 1)
                if p >= 4:
                    for t in range(NT):
                        n = 3 * (p - 4) + t
                        act.wait_ge(evac, done(p, t))
                        if 6 <= p < 10:
                            act.wait_ge(vt_pe, 3 * (p - 5))
                        if p >= 10:
                            act.wait_ge(mix_mul, 3 * (p - 9))
                        nc.scalar.activation(gelu[p % 2][:, t * TT:(t + 1) * TT], tmp[t][:, :],
                                             ACT.Gelu_apprx_tanh).then_inc(gelued, 1)
                        if p >= 8:
                            c = p - 8
                            buf, m = (hr, c) if c < 4 else (spatial, c - 4)
                            ch = 4 + c if c < 4 else c - 4
                            act.wait_ge(mix_mul, 3 * c + t + 1)
                            nc.scalar.copy(pt(h_hi, ch, t), buf[:, m, t * TT:(t + 1) * TT]).then_inc(mix_high, 1)
                if p in (2, 4, 6, 8):
                    j = p // 2 - 1
                    for o in range(2):
                        g = 1 - o
                        for t in range(3):
                            n = 6 * j + 3 * o + t
                            act.wait_ge(gate_pe, n + 1)
                            if t == 0 and j > 0:
                                if o == 0:
                                    act.wait_ge(lru_pool, 3 * j)
                                else:
                                    act.wait_ge(scanned, 2 * j)
                            dst = (q, ig)[g]
                            nc.scalar.activation(dst[:, t * LT:(t + 1) * LT], ps[:, M0 + n % 2, 0:LT], ACT.Sigmoid,
                                                 bias=vec(V_BIAS + (1 + g) * HC + j)).then_inc(gate_act, 1)

            out_squares(0, EVEN_OUT)
            end_phase(0, MLP[0])
            mlp(0, 1, ODD_IN)

            def odd_pad(c, q):
                act.wait_ge(czeros, 2)
                wait(act, cconv, 3 * c - 3)
                nc.scalar.copy(cp[q][:, PS:PS + CC - 1].unsqueeze(2), cache_c[:, :, ds(c, 1)]).then_inc(cpad_in, 1)

            def odd_tail(c, q):
                act.wait_ge(cp_ok, 4 * c + 4)
                nc.scalar.copy(tail_c[:, 0, :, ds(c, 1)], cp[q][:, SEQ:SEQ + CC - 1].unsqueeze(2)).then_inc(ctails, 1)
                nc.scalar.copy(tail_c[:, 1, :, ds(c, 1)], cp[q][:, PB - (CC - 1):PB].unsqueeze(2)).then_inc(ctails, 1)

            def odd_high(c, q):
                for t in range(NT):
                    for j, (o0, n, tok, smp) in enumerate(tile_pieces(t)):
                        act.wait_ge(mix_mul, 24 + 4 * c + t + j + 1)
                        y = cy[q][:, (PS if smp else tok):(PS if smp else tok) + n]
                        nc.scalar.copy(h_hi[:, ds(c * TOK + tok, n)], y).then_inc(mix_high, 1)

            def odd_panel(i, k, has_high=True, has_gain=True):
                p, c, q = ODD_IN + 6 * i + k, 2 * i + k // 3, k // 3
                if has_high:
                    high(p + 1, 1 - k % 2, ODD_IN // 2 + 3 * i + (k + 1) // 2 + 1, 48 + 6 * i + k + 1 if has_gain else None)
                if k % 3 == 0:
                    odd_pad(c, q)
                if k % 3 == 1:
                    odd_tail(c, q)
                if k % 3 == 2:
                    odd_high(c, q)

            high_of(ODD_IN + 2, True)
            for t in range(NT):
                rs_root(pre_n(2, t))
                rs_copy(pre_n(2, t), t)
            odd_pad(0, 0)
            odd_tail(0, 0)
            for k in range(2, 6):
                odd_panel(0, k)
            with act.Fori(1, KC // 2 - 1) as i:
                for k in range(6):
                    odd_panel(i, k)
            for k in range(6):
                odd_panel(KC // 2 - 1, k, has_gain=k < 5)
            out_squares(2, ODD_OUT)
            end_phase(2, MLP[1])
            mlp(1, 3)

            act.wait_ge(t_pe, 1)
            nc.scalar.copy(tail_rows[:, :], ps[0:T_COLS, M0, 0:P]).then_inc(t_ok, 1)
            for n in range(9):
                w = P if n < 8 else DEC
                dst = y_rows[:, n, 512:D] if n < 8 else y_rows_s[:, 512:D]
                act.wait_ge(y_pe, 2 * n + 2)
                nc.scalar.copy(dst, ps[0:w, 2 * (n % 3) + 1, :]).then_inc(y_b, 1)

        @block.vector
        def _(dve):
            steps = [0]

            def link(ins):
                ins.then_inc(soft_ok, 1)
                steps[0] += 1
                dve.wait_ge(soft_ok, steps[0])

            def softplus():
                dve.wait_ge(soft_act, 2)
                e, z, z2, poly = soft[:, 1, :], soft[:, 2, :], soft[:, 3, :], soft[:, 4, :]
                link(nc.vector.tensor_scalar(soft[:, 0, :], e, 2.0, None, ALU.add))
                link(nc.vector.reciprocal(soft[:, 5, :], soft[:, 0, :]))
                link(nc.vector.tensor_tensor(z, e, soft[:, 5, :], ALU.mult))
                link(nc.vector.tensor_tensor(z2, z, z, ALU.mult))
                link(nc.vector.tensor_scalar(poly, z2, 1.0 / 15, 1.0 / 13, ALU.mult, ALU.add))
                for odd in (11, 9, 7, 5, 3, 1):
                    link(nc.vector.tensor_tensor(poly, poly, z2, ALU.mult))
                    link(nc.vector.tensor_scalar(poly, poly, 1.0 / odd, None, ALU.add))
                link(nc.vector.tensor_tensor(poly, poly, z, ALU.mult))
                link(nc.vector.tensor_scalar(soft[:, 6, :], vecs[:, V_LAMBDA:V_LAMBDA + HC], -1.0, 0.0, ALU.mult,
                                             ALU.max))
                link(nc.vector.scalar_tensor_tensor(soft[:, 6, :], poly, 2.0, soft[:, 6, :], ALU.mult, ALU.add))
                link(nc.vector.tensor_scalar(soft[:, 7, :], soft[:, 6, :], 4.0, None, ALU.mult))
                link(nc.vector.tensor_scalar(soft[:, 8, :], soft[:, 6, :], -8.0, None, ALU.mult))
                assert steps[0] == SOFT_STEPS

            def low(p, s, load=None, gained=None):
                dve.wait_ge(w_high, p + 1)
                nc.vector.tensor_tensor(w_lo[s][:, :], w_raw[s][:, :], w_hi[s][:, :].bitcast(F32),
                                        ALU.subtract).then_inc(w_ready, 1)

            def low_of(p):
                low(p, p % 2)

            def factors(n, t):
                dve.wait_ge(rooted, n + 1)
                wait(dve, diag, n)
                nc.vector.reciprocal(rcol[0:JW, :], root[0:JW, :]).then_inc(inverted, 1)
                dve.wait_ge(inverted, n + 1)
                nc.vector.tensor_tensor(tmp[t][0:JW, :].rearrange("p (j c) -> p j c", j=NJ),
                                        ident[0:JW, 0:JW].unsqueeze(1).to_broadcast([JW, NJ, JW]),
                                        rcol[0:JW, :].unsqueeze(2).to_broadcast([JW, NJ, JW]),
                                        ALU.mult).then_inc(diag, 1)

            def scaled(dst, p, s, t):
                dve.wait_ge(pe_tile, done(p, t))
                return nc.vector.tensor_tensor(dst, bank(s, t), rstd[:, t * TT:(t + 1) * TT], ALU.mult)

            def sum_squares(u, t):
                if u == 0 and t == 0:
                    dve.wait_ge(x0_sq, KC)
                else:
                    dve.wait_ge(upd_act, 2 * (24 * u + 8 * t + KC))
                squares = f[:, :].rearrange("p (k n) -> p n k", k=KC)[:, t * TT:(t + 1) * TT, :]
                nc.vector.tensor_reduce(sq_sum[:, t * TT:(t + 1) * TT], squares, mybir.AxisListType.X, ALU.add
                                        ).then_inc(acc_dve, 1)

            def x_low(u, t, k):
                dve.wait_ge(upd_act, 2 * (24 * u + 8 * t + k + 1))
                if u == 0 and t == 0:
                    dve.wait_ge(x0_sq, k + 1)
                nc.vector.tensor_tensor(pt(x_lo, k, t), pt(x_sum, k, t), pt(x_hi, k, t).bitcast(F32),
                                        ALU.subtract).then_inc(x_ready, 1)

            def update(b, t, k0=0, k1=KC):
                if k0 == 0:
                    dve.wait_ge(rs_ready, post_n(b, t) + 1)
                for k in range(k0, k1 if k1 < KC else KC + 2):
                    if k < KC:
                        nc.vector.scalar_tensor_tensor(pt(f, k, t), pt(f, k, t),
                                                       vec(V_GAIN + POST_GAIN[b] * KC + k),
                                                       rstd[:, t * TT:(t + 1) * TT], ALU.mult, ALU.mult
                                                       ).then_inc(upd_a, 1)
                    if k >= 2 and b < 3:
                        x_low(b + 1, t, k - 2)

            def add_out(n, p, s, m, t, copy, stat):
                dve.wait_ge(pe_tile, done(p, t))
                if copy:
                    nc.vector.tensor_copy(pt(f, m, t), bank(s, t)).then_inc(evac, 1)
                else:
                    dve.wait_ge(evac, 3 * p - 45)
                    nc.vector.tensor_tensor(pt(f, m, t), bank(s, t), pt(f, m, t), ALU.add).then_inc(evac, 1)
                if stat:
                    dst = sq_sum[:, t * TT:(t + 1) * TT]
                    dve.wait_ge(f_sq, n + 1)
                    if isinstance(m, int) and m == 0:
                        nc.vector.tensor_copy(dst, tmp[t][:, :]).then_inc(f_acc, 1)
                    else:
                        dve.wait_ge(f_acc, n - 1 if isinstance(p, int) and p - p % 2 in PAIRED else n - 2)
                        nc.vector.tensor_tensor(dst, dst, tmp[t][:, :], ALU.add).then_inc(f_acc, 1)

            def out_chunks(b, base, copy):
                def work(p, s, c):
                    for t in range(NT):
                        add_out(24 * b + 3 * c + t, p, s, c, t, copy, True)

                low_of(base + 1)
                work(base, 0, 0)
                low_of(base + 2)
                work(base + 1, 1, 1)
                slots(dve, base, 2, 6, low, work, (None, None))

            def end_phase(b, copy, next_panel=None):
                p = LAST[b] - 1

                def add_pair(t, s):
                    add_out(24 * b + 18 + 2 * t + s, p + s, s, 6 + s, t, copy, True)

                low_of(p + 1)
                add_pair(0, 0)
                add_pair(0, 1)
                factors(post_n(b, 0), 0)
                add_pair(1, 0)
                update(b, 0, 0, 2)
                add_pair(1, 1)
                update(b, 0, 2, 4)
                factors(post_n(b, 1), 1)
                update(b, 0, 4, 8)
                if b < 3:
                    low_of(next_panel)
                add_pair(2, 0)
                update(b, 1, 0, 2)
                add_pair(2, 1)
                if b < 3:
                    low_of(next_panel + 1)
                update(b, 1, 2, 4)
                factors(post_n(b, 2), 2)
                update(b, 1, 4, 8)
                update(b, 2)

            def begin_phase(u, base, evacuate):
                sum_squares(u, 0)
                low_of(base + 2)
                for t in range(NT):
                    factors(pre_n(u, t), t)
                    if t == 1:
                        sum_squares(u, 2)
                    dve.wait_ge(rs_ready, pre_n(u, t) + 1)
                    for s in range(2):
                        evacuate(base + s, s, t)

            def relu(n, p, s, c, t):
                dve.wait_ge(pe_tile, done(p, t))
                wait(dve, h_ready, n if isinstance(p, int) and p - p % 2 in PAIRED else n - 2)
                nc.vector.scalar_tensor_tensor(tmp[t][:, :], bank(s, t), 0.0, rstd[:, t * TT:(t + 1) * TT],
                                               ALU.max, ALU.mult).then_inc(evac, 1)
                dve.wait_ge(h_high, n + 1)
                nc.vector.tensor_tensor(pt(h_lo, c, t), tmp[t][:, :], pt(h_hi, c, t).bitcast(F32),
                                        ALU.subtract).then_inc(h_ready, 1)

            def mlp(l, u, next_panel=None):
                for g in range(GROUPS):
                    base = MLP[l] + 16 * g
                    n0 = 96 * l + 24 * g

                    def up(p, s, c, n0=n0):
                        for t in range(NT):
                            relu(n0 + 3 * c + t, p, s, c, t)

                    def down(p, s, c, g=g):
                        for t in range(NT):
                            add_out(None, p, s, c, t, g == 0, False)

                    if g == 0:
                        begin_phase(u, base, lambda p, s, t, n0=n0: relu(n0 + 2 * t + s, p, s, s, t))
                    slots(dve, base, 2 if g == 0 else 0, 8, low, up, (None, None))
                    if g < GROUPS - 1:
                        slots(dve, base + 8, 0, 8, low, down, (None, None))
                out_chunks(2 * l + 1, MLP[l] + 56, False)
                end_phase(2 * l + 1, False, next_panel)

            xk = x_sum[:, :].rearrange("p (k n) -> p k n", k=KC)
            for n in range(SEQ // P):
                dve.wait_ge(x0_t, n + 1)
                nc.vector.tensor_copy(xk[:, 0:4, n * P:(n + 1) * P],
                                      ps[:, 2 * (n % 3), :].rearrange("p (k n) -> p k n", k=4)).then_inc(x0_a, 1)
                if n == 5:
                    for k in range(KC):
                        x_low(0, 0, k)
            dve.wait_ge(x0_t, 9)
            nc.vector.tensor_copy(xk[:, :, SEQ:TOK],
                                  ps[:, M0, 0:KC * DEC].rearrange("p (k n) -> p k n", k=KC)).then_inc(x0_a, 1)
            low_of(0)
            low_of(1)
            for t in (1, 2):
                for k in range(KC):
                    x_low(0, t, k)

            xc, q, ig, rc = lru

            def xb_out(p, s, t):
                dve.wait_ge(pe_tile, done(p, t))
                dve.wait_ge(zeros, 2)
                for j, (o0, n, tok, smp) in enumerate(tile_pieces(t)):
                    dst = LS + CB - 1 if smp else CB - 1 + tok
                    ins = nc.vector.tensor_tensor(xb_pad[:, p, dst:dst + n], ps[:, s * NT + t, o0:o0 + n],
                                                  rstd[:, tok:tok + n], ALU.mult)
                ins.then_inc(evac, 1)

            def convolve(j):
                if j == 0:
                    dve.wait_ge(pad_in, 1)
                else:
                    dve.wait_ge(lru_pool, 3 * j - 2)
                dve.wait_ge(evac, done(j, 2))
                nc.vector.tensor_scalar(xc[:, :], xb_pad[:, j, 0:LV], vec(V_CONV_B + j), vec(V_BIAS + j),
                                        ALU.mult, ALU.add).then_inc(conv, 1)
                for r in range(1, CB):
                    dve.wait_ge(conv, 4 * j + r)
                    nc.vector.scalar_tensor_tensor(xc[:, :], xb_pad[:, j, r:r + LV], vec(V_CONV_B + r * HC + j),
                                                   xc[:, :], ALU.mult, ALU.add).then_inc(conv, 1)

            def decay(j):
                dve.wait_ge(lru_act, 3 * j + 1)
                nc.vector.tensor_scalar(rc[:, :], rc[:, :], 0.5, 0.5, ALU.mult, ALU.add).then_inc(lru_dve, 1)
                dve.wait_ge(lru_dve, 4 * j + 1)
                dve.wait_ge(lru_act, 3 * j + 2)
                nc.vector.scalar_tensor_tensor(lru_t[:, :], q[:, :], 1.0, rc[:, :], ALU.add, ALU.mult
                                               ).then_inc(lru_dve, 1)
                dve.wait_ge(lru_dve, 4 * j + 2)
                nc.vector.scalar_tensor_tensor(lru_t[:, :], lru_t[:, :], 2.0, rc[:, :], ALU.subtract, ALU.mult,
                                               reverse0=True).then_inc(lru_dve, 1)
                dve.wait_ge(lru_dve, 4 * j + 3)
                nc.vector.tensor_scalar(rc[:, :], lru_t[:, :], 2.0, -1.0, ALU.mult, ALU.add).then_inc(lru_dve, 1)

            def scan(j):
                dve.wait_ge(lru_dve, 4 * j + 4)
                dve.wait_ge(lru_pool, 3 * j + 3)
                nc.vector.tensor_tensor_scan(hr[:, j, 0:SEQ], rc[:, 0:SEQ], q[:, 0:SEQ], 0.0, ALU.mult,
                                             ALU.add).then_inc(scanned, 1)
                nc.vector.tensor_tensor_scan(hr[:, j, SEQ:TOK], rc[:, LS:LS + DEC], q[:, LS:LS + DEC],
                                             vec(V_H0 + j), ALU.mult, ALU.add).then_inc(scanned, 1)

            begin_phase(0, EVEN_IN, xb_out)
            convolve(0)
            for p in range(2, 16):
                low_of(p + 1)
                if p >= 5:
                    dve.wait_ge(gelued, 3 * (p - 4))
                for t in range(NT):
                    if p in (4, 6, 8) and t == 2:
                        convolve(p // 2 - 1)
                    if p < 4:
                        xb_out(p, p % 2, t)
                    else:
                        scaled(tmp[t][:, :], p, p % 2, t).then_inc(evac, 1)
                if p == 2:
                    softplus()
                if p in (3, 5, 7, 9):
                    decay((p - 3) // 2)
                if p in (4, 6, 8, 10):
                    scan(p // 2 - 2)
                if p == 10:
                    dve.wait_ge(v_rt, 2)
                    dve.wait_ge(s_in, 32)
                    nc.vector.reciprocal(v_rstd[:, 0:8], v_root[:, 0:8]).then_inc(v_inv, 1)
                    nc.vector.reciprocal(v_rstd[0:DEC, 8:9], v_root[0:DEC, 8:9]).then_inc(v_inv, 1)
                    dve.wait_ge(v_inv, 2)
                    for n in range(9):
                        rows = P if n < 8 else DEC
                        v = v_tok[:, n, :] if n < 8 else v_tok_s[:, :]
                        nc.vector.scalar_tensor_tensor(v, v, v_rstd[0:rows, n:n + 1], v_gain_bc[0:rows, :], ALU.mult,
                                                       ALU.mult).then_inc(v_ok, 1)
                if p == 11:
                    dve.wait_ge(b_in, 16)
                    for h in range(HC):
                        for part in range(3):
                            n = 3 * h + part
                            dve.wait_ge(sgu_pe, n + 1)
                            b = M0 + n % 2
                            if part < 2:
                                nc.vector.tensor_tensor(
                                    spatial[:, h, part * 512:(part + 1) * 512].rearrange("p (n i) -> p n i", n=4),
                                    ps[:, b, :].rearrange("p (n i) -> p n i", n=4),
                                    bias_bc[:, h:h + 1, :].to_broadcast([P, 4, P]), ALU.add).then_inc(sgu_ok, 1)
                            else:
                                nc.vector.tensor_tensor(spatial[:, h, SEQ:TOK], ps[:, b, 0:DEC], bias_bc[:, h, 0:DEC],
                                                        ALU.add).then_inc(sgu_ok, 1)

            out_chunks(0, EVEN_OUT, True)
            end_phase(0, True, MLP[0])
            mlp(0, 1, ODD_IN)

            def odd_out(p, s, c, q, kind, t):
                if kind == 0:
                    wait(dve, cp_ok, 4 * c - 4)
                    scaled(cg[q][:, t * TT:(t + 1) * TT], p, s, t).then_inc(evac, 1)
                elif kind == 1:
                    dve.wait_ge(mix_mul, 24 + 4 * c)
                    scaled(tmp[t][:, :], p, s, t).then_inc(evac, 1)
                else:
                    dve.wait_ge(cp_ok, 4 * c + 4)
                    scaled(tmp[t][:, :], p, s, t).then_inc(evac, 1)

            def odd_convolve(c, q):
                dve.wait_ge(cp_ok, 4 * c + 4)
                dve.wait_ge(cpad_in, c + 1)
                dve.wait_ge(mix_ready, 24 + 4 * c - (0 if isinstance(c, int) and c == 0 else 4))
                nc.vector.tensor_scalar(cy[q][:, :], cp[q][:, 0:PV], vec(V_CONV_C + c), None,
                                        ALU.mult).then_inc(cconv, 1)
                for r in range(1, CC):
                    dve.wait_ge(cconv, 3 * c + r)
                    nc.vector.scalar_tensor_tensor(cy[q][:, :], cp[q][:, r:r + PV], vec(V_CONV_C + r * KC + c),
                                                   cy[q][:, :], ALU.mult, ALU.add).then_inc(cconv, 1)

            def odd_panel(i, k):
                p, c, q, kind = ODD_IN + 6 * i + k, 2 * i + k // 3, k // 3, k % 3
                low(p + 1, 1 - k % 2)
                for t in range(NT):
                    odd_out(p, k % 2, c, q, kind, t)
                if kind == 1:
                    odd_convolve(c, q)

            begin_phase(2, ODD_IN, lambda p, s, t: odd_out(p, s, 0, 0, s, t))
            odd_convolve(0, 0)
            for k in range(2, 6):
                odd_panel(0, k)
            with dve.Fori(1, KC // 2) as i:
                for k in range(6):
                    odd_panel(i, k)
            out_chunks(2, ODD_OUT, True)
            end_phase(2, True, MLP[1])
            mlp(1, 3)

            for n in range(9):
                w = P if n < 8 else DEC
                dst = y_rows[:, n, 0:512] if n < 8 else y_rows_s[:, 0:512]
                dve.wait_ge(y_pe, 2 * n + 1)
                nc.vector.tensor_copy(dst, ps[0:w, 2 * (n % 3), :]).then_inc(y_a, 1)


VEC_SRC = [("norm_mix_pre", 2 * KC), ("norm_ffn_pre", 2 * KC), ("norm_mix_post", 2 * KC), ("norm_ffn_post", 2 * KC),
           ("b_conv_w", CB * HC), ("b_conv_b", HC), ("b_ba", HC), ("b_bx", HC), ("b_lambda", HC), ("state_b_h", HC),
           ("c_conv_w", CC * KC), ("cache_b_conv", (CB - 1) * HC), ("cache_c_conv", (CC - 1) * KC)]
CACHE_ROWS = (CB - 1) * HC + (CC - 1) * KC
SOFT_STEPS = 5 + 12 + 5

_INS = ['x_prompt', 'x_sample', 'cache_b_conv', 'state_b_h', 'cache_c_conv', 'norm_mix_pre', 'norm_mix_post',
        'norm_ffn_pre', 'norm_ffn_post', 'w_in_even', 'a_v_gain', 'a_w_s', 'a_b_s', 'b_conv_w', 'b_conv_b', 'b_wa',
        'b_ba', 'b_wx', 'b_bx', 'b_lambda', 'w_out_even', 'c_w_in', 'c_conv_w', 'c_w_out', 'mlp_up', 'mlp_down']
_OUTS = [("y_prompt", (1, SEQ, D)), ("y_sample", (1, DEC, D)), ("v", (1, 1, DEC, HALF)),
         ("bconv_p", (1, 1, CB - 1, HALF)), ("bh_p", (1, 1, HALF)), ("cconv_p", (1, 1, CC - 1, D)),
         ("bconv_s", (1, 1, CB - 1, HALF)), ("bh_s", (1, 1, HALF)), ("cconv_s", (1, 1, CC - 1, D))]


def kernel(**inputs):
    import numpy as _np
    import concourse.bacc as _bacc
    from concourse import mybir as _mybir
    from concourse.bass_utils import run_bass_kernel_spmd as _run

    nc = _bacc.Bacc("TRN2", target_bir_lowering=False, num_devices=1)
    arrays, ins, outs = {}, {}, {}
    for name in _INS:
        a = _np.ascontiguousarray(inputs[name])
        arrays[f"in_{name}_dram"] = a
        ins[name] = nc.dram_tensor(f"in_{name}_dram", a.shape, _mybir.dt.from_np(a.dtype), kind="ExternalInput").ap()
    for name, shape in _OUTS:
        outs[name] = nc.dram_tensor(f"out_{name}_dram", shape, _mybir.dt.float32, kind="ExternalOutput").ap()
    build(nc, ins, outs)
    r = _run(nc, [arrays], core_ids=[0])
    return tuple(r.results[0][f"out_{name}_dram"] for name, _ in _OUTS)
```
